# Optimizing a Trainium2 kernel written in Bass

```python
import jax, jax.numpy as jnp
from jax import lax
import numpy as np

D_MODEL = 2048
BATCH = 1
SEQ = 256
DEPTH = 1

ATT_HEADS = 16
ATT_KV_HEADS = 2
HEAD_DIM = 64
ATT_WIDTH = ATT_HEADS * HEAD_DIM
KV_WIDTH = ATT_KV_HEADS * HEAD_DIM
GROUP = ATT_HEADS // ATT_KV_HEADS
WINDOW = 128
BLOCK = 128
ROT_DIM = HEAD_DIM // 4
ROPE_THETA = 500000.0
HG_HEADS = 8
HG_EXPAND = 128
HG_HEAD_V = 128
HG_F_WIDTH = HG_HEADS * HG_EXPAND
HG_V_WIDTH = HG_HEADS * HG_HEAD_V
CHUNK = 64
N_LB = DEPTH + 1
FFN_HIDDEN = ((8 * D_MODEL // 3 + 255) // 256) * 256
N_MOD = 6
IN_COLS = ATT_WIDTH + 2 * KV_WIDTH + 2 * HG_F_WIDTH + 2 * HG_V_WIDTH + 2 * D_MODEL
EPS = 1e-6


def rmsnorm(t, gain):
    t32 = t.astype(jnp.float32)
    y = t32 * lax.rsqrt(jnp.mean(t32 * t32, axis=-1, keepdims=True) + EPS)
    return (y * gain.astype(jnp.float32)).astype(t.dtype)

def rope_partial(t, cos, sin):
    half = ROT_DIM // 2
    t1 = t[..., :half].astype(jnp.float32)
    t2 = t[..., half:ROT_DIM].astype(jnp.float32)
    rot = jnp.concatenate([t1 * cos - t2 * sin, t2 * cos + t1 * sin], axis=-1)
    return jnp.concatenate([rot.astype(t.dtype), t[..., ROT_DIM:]], axis=-1)

def sliding_window_attention(q, k, v, sinks):
    B, S = q.shape[0], q.shape[1]
    nb = S // BLOCK
    qb = q.reshape(B, nb, BLOCK, ATT_KV_HEADS, GROUP, HEAD_DIM).astype(jnp.float32)
    kb = k.reshape(B, nb, BLOCK, ATT_KV_HEADS, HEAD_DIM).astype(jnp.float32)
    vb = v.reshape(B, nb, BLOCK, ATT_KV_HEADS, HEAD_DIM).astype(jnp.float32)
    prev = lambda t: jnp.concatenate([jnp.zeros_like(t[:, :1]), t[:, :-1]], axis=1)
    kk = jnp.concatenate([prev(kb), kb], axis=2)
    vv = jnp.concatenate([prev(vb), vb], axis=2)
    logits = jnp.einsum('bnqhgd,bnkhd->bnhgqk', qb, kk) * (HEAD_DIM ** -0.5)
    qi = jnp.arange(BLOCK)[:, None]
    kj = jnp.arange(2 * BLOCK)[None, :]
    rel = BLOCK + qi - kj
    band = (rel >= 0) & (rel < WINDOW)
    has_prev = (jnp.arange(nb) > 0)[:, None, None] | (kj >= BLOCK)[None]
    mask = band[None] & has_prev
    logits = jnp.where(mask[None, :, None, None], logits, -jnp.inf)
    sink = sinks.astype(jnp.float32).reshape(ATT_KV_HEADS, GROUP)[None, None, :, :, None, None]
    m = jnp.maximum(jnp.max(logits, axis=-1, keepdims=True), sink)
    p = jnp.exp(logits - m)
    denom = jnp.sum(p, axis=-1, keepdims=True) + jnp.exp(sink - m)
    out = jnp.einsum('bnhgqk,bnkhd->bnqhgd', p / denom, vv)
    return out.reshape(B, S, ATT_WIDTH).astype(q.dtype)

def hgrn2_recurrence(q, f_raw, i, lb):
    B, S = q.shape[0], q.shape[1]
    nc = S // CHUNK
    f = lb + (1.0 - lb) * jax.nn.sigmoid(f_raw.astype(jnp.float32))
    key = 1.0 - f
    logf = jnp.log(f)

    def chunks(t, d):
        return t.astype(jnp.float32).reshape(B, nc, CHUNK, HG_HEADS, d).transpose(1, 0, 3, 2, 4)

    qc = chunks(jax.nn.silu(q.astype(jnp.float32)), HG_EXPAND)
    kc = chunks(key, HG_EXPAND)
    vc = chunks(i, HG_HEAD_V)
    bc = jnp.cumsum(chunks(logf, HG_EXPAND), axis=3)
    causal = jnp.tril(jnp.ones((CHUNK, CHUNK), dtype=bool))[:, :, None]

    def step(state, xs):
        qt, kt, vt, bt = xs
        o_inter = jnp.einsum('bhck,bhkv->bhcv', qt * jnp.exp(bt), state)
        diff = bt[:, :, :, None, :] - bt[:, :, None, :, :]
        decay = jnp.where(causal, jnp.exp(jnp.where(causal, diff, 0.0)), 0.0)
        scores = jnp.einsum('bhtk,bhtsk,bhsk->bhts', qt, decay, kt)
        o = o_inter + jnp.einsum('bhts,bhsv->bhtv', scores, vt)
        b_last = bt[:, :, -1:, :]
        new_state = (jnp.exp(b_last[:, :, 0, :])[..., None] * state
                     + jnp.einsum('bhsk,bhsv->bhkv', kt * jnp.exp(b_last - bt), vt))
        return new_state, o

    state0 = jnp.zeros((B, HG_HEADS, HG_EXPAND, HG_HEAD_V), jnp.float32)
    _, o = lax.scan(step, state0, (qc, kc, vc, bc))
    return o.transpose(1, 0, 3, 2, 4).reshape(B, S, HG_HEADS, HG_HEAD_V)

def first_inputs(seed: int = 0) -> dict:
    key = jax.random.key(seed)
    ks = jax.random.split(key, 20)
    f32 = jnp.float32
    nrm = lambda k, shape, scale: (jax.random.normal(k, shape, f32) * scale)
    gain = lambda k, shape: 1.0 + 0.05 * jax.random.normal(k, shape, f32)
    offsets = jax.random.randint(ks[2], (BATCH, 1), 0, 4096, dtype=jnp.int32)
    positions = (offsets + jnp.arange(SEQ, dtype=jnp.int32)[None, :]).astype(jnp.int32)
    return {
        "x": nrm(ks[0], (BATCH, SEQ, D_MODEL), 1.0),
        "c": nrm(ks[1], (BATCH, D_MODEL), 1.0),
        "positions": positions,
        "w_ada": nrm(ks[3], (DEPTH, D_MODEL, N_MOD * D_MODEL), 0.5 * D_MODEL ** -0.5),
        "b_ada": nrm(ks[4], (DEPTH, N_MOD * D_MODEL), 0.02),
        "g_pre_mix": gain(ks[5], (DEPTH, D_MODEL)),
        "g_post_mix": gain(ks[6], (DEPTH, D_MODEL)),
        "g_pre_ffn": gain(ks[7], (DEPTH, D_MODEL)),
        "g_post_ffn": gain(ks[8], (DEPTH, D_MODEL)),
        "w_in": nrm(ks[9], (DEPTH, D_MODEL, IN_COLS), D_MODEL ** -0.5),
        "attn_sinks": nrm(ks[10], (DEPTH, ATT_HEADS), 1.0),
        "w_attn_proj": nrm(ks[11], (DEPTH, ATT_WIDTH, D_MODEL), ATT_WIDTH ** -0.5),
        "hg_lower_bounds": nrm(ks[12], (N_LB, HG_F_WIDTH), 0.5),
        "hg_norm": gain(ks[13], (DEPTH, HG_HEAD_V)),
        "w_hgrn_proj": nrm(ks[14], (DEPTH, HG_V_WIDTH, D_MODEL), HG_V_WIDTH ** -0.5),
        "w_out": nrm(ks[15], (DEPTH, D_MODEL, D_MODEL), D_MODEL ** -0.5),
        "w_ffn_in": nrm(ks[16], (DEPTH, D_MODEL, 2 * FFN_HIDDEN), D_MODEL ** -0.5),
        "w_ffn_out": nrm(ks[17], (DEPTH, FFN_HIDDEN, D_MODEL), FFN_HIDDEN ** -0.5),
    }

def first_block(x, c, positions, w_ada, b_ada, g_pre_mix, g_post_mix, g_pre_ffn, g_post_ffn,
              w_in, attn_sinks, w_attn_proj, hg_lower_bounds, hg_norm, w_hgrn_proj, w_out,
              w_ffn_in, w_ffn_out):
    B, S = x.shape[0], x.shape[1]
    inv_freq = ROPE_THETA ** (-jnp.arange(0, ROT_DIM, 2, dtype=jnp.float32) / ROT_DIM)
    ang = positions.astype(jnp.float32)[..., None] * inv_freq
    cos, sin = jnp.cos(ang)[:, :, None, :], jnp.sin(ang)[:, :, None, :]
    lb_table = jnp.cumsum(jax.nn.softmax(hg_lower_bounds.astype(jnp.float32), axis=0), axis=0)
    splits = [ATT_WIDTH, ATT_WIDTH + KV_WIDTH, ATT_WIDTH + 2 * KV_WIDTH,
              ATT_WIDTH + 2 * KV_WIDTH + HG_F_WIDTH,
              ATT_WIDTH + 2 * KV_WIDTH + 2 * HG_F_WIDTH,
              ATT_WIDTH + 2 * KV_WIDTH + 2 * HG_F_WIDTH + HG_V_WIDTH,
              ATT_WIDTH + 2 * KV_WIDTH + 2 * HG_F_WIDTH + 2 * HG_V_WIDTH,
              ATT_WIDTH + 2 * KV_WIDTH + 2 * HG_F_WIDTH + 2 * HG_V_WIDTH + D_MODEL]
    for l in range(DEPTH):
        mod = (c @ w_ada[l] + b_ada[l])[:, None, :]
        shift1, scale1, gate1, shift2, scale2, gate2 = jnp.split(mod, N_MOD, axis=-1)

        h = rmsnorm(x, g_pre_mix[l]) * (1.0 + scale1) + shift1
        proj = h @ w_in[l]
        q_a, k_a, v_a, q_h, f_h, i_h, g_h, gate_a, gate_h = jnp.split(proj, splits, axis=-1)
        qa = rope_partial(q_a.reshape(B, S, ATT_HEADS, HEAD_DIM), cos, sin)
        ka = rope_partial(k_a.reshape(B, S, ATT_KV_HEADS, HEAD_DIM), cos, sin)
        va = v_a.reshape(B, S, ATT_KV_HEADS, HEAD_DIM)
        y_a = sliding_window_attention(qa, ka, va, attn_sinks[l]) @ w_attn_proj[l]
        o_h = hgrn2_recurrence(q_h, f_h, i_h, lb_table[l])
        o_h = rmsnorm(o_h, hg_norm[l]).reshape(B, S, HG_V_WIDTH).astype(x.dtype)
        y_h = (o_h * jax.nn.sigmoid(g_h)) @ w_hgrn_proj[l]
        merged = jax.nn.sigmoid(gate_a) * y_a + jax.nn.sigmoid(gate_h) * y_h
        y = merged @ w_out[l]
        x = x + gate1 * rmsnorm(y, g_post_mix[l])

        h = rmsnorm(x, g_pre_ffn[l]) * (1.0 + scale2) + shift2
        gu = h @ w_ffn_in[l]
        g_ffn, u_ffn = jnp.split(gu, 2, axis=-1)
        y = (jax.nn.silu(g_ffn) * u_ffn) @ w_ffn_out[l]
        x = x + gate2 * rmsnorm(y, g_post_ffn[l])
    return x


DEPTH_2 = 2

N_MIXERS = 2
GRID_W = 64
N_META = 16
NORM_EPS = 1e-6

ATTN_HEADS = 16
ATTN_KV_HEADS = 8
ATTN_GROUP = ATTN_HEADS // ATTN_KV_HEADS
ATTN_HEAD_DIM = 128
ATTN_WIDTH = ATTN_HEADS * ATTN_HEAD_DIM
ATTN_KV_WIDTH = ATTN_KV_HEADS * ATTN_HEAD_DIM
ATTN_IN = 2 * ATTN_WIDTH + 2 * ATTN_KV_WIDTH
Q_BLOCK = 128
ROPE_THETA_2 = 10000.0
ROPE_AXIS_DIM = ATTN_HEAD_DIM // 2

GLA_HEADS = 4
GLA_KEY_DIM = D_MODEL // 2
GLA_VALUE_DIM = D_MODEL
GLA_HEAD_K = GLA_KEY_DIM // GLA_HEADS
GLA_HEAD_V = GLA_VALUE_DIM // GLA_HEADS
GLA_GATE_RANK = 16
GLA_GATE_NORMALIZER = 16.0
GLA_CHUNK = 64
GLA_IN = 2 * GLA_KEY_DIM + 2 * GLA_VALUE_DIM + 2 * GLA_GATE_RANK

N_ATTN_LAYERS = (DEPTH_2 + 1) // 2
N_GLA_LAYERS = DEPTH_2 // 2


def rmsnorm_2(x, w):
    xf = x.astype(jnp.float32)
    y = xf * lax.rsqrt(jnp.mean(xf * xf, axis=-1, keepdims=True) + NORM_EPS)
    return (y * w.astype(jnp.float32)).astype(x.dtype)

def axial_rope_angles(seq_len):
    rows = seq_len // GRID_W
    row = jnp.repeat(jnp.arange(rows), GRID_W).astype(jnp.float32)
    col = jnp.tile(jnp.arange(GRID_W), rows).astype(jnp.float32)
    inv_freq = ROPE_THETA_2 ** (-jnp.arange(0, ROPE_AXIS_DIM, 2, dtype=jnp.float32) / ROPE_AXIS_DIM)
    meta = jnp.zeros((N_META, ROPE_AXIS_DIM // 2), jnp.float32)
    ang_row = jnp.concatenate([meta, row[:, None] * inv_freq[None]], axis=0)
    ang_col = jnp.concatenate([meta, col[:, None] * inv_freq[None]], axis=0)
    return ang_row, ang_col

def _rotate(x, ang):
    cos = jnp.cos(ang)[None, :, None, :].astype(x.dtype)
    sin = jnp.sin(ang)[None, :, None, :].astype(x.dtype)
    x1, x2 = jnp.split(x, 2, axis=-1)
    return jnp.concatenate([x1 * cos - x2 * sin, x2 * cos + x1 * sin], axis=-1)

def apply_axial_rope(x, ang_row, ang_col):
    return jnp.concatenate([_rotate(x[..., :ROPE_AXIS_DIM], ang_row),
                            _rotate(x[..., ROPE_AXIS_DIM:], ang_col)], axis=-1)

def _attend(qb, k, v):
    s = jnp.einsum('bqkgd,bskd->bkgqs', qb, k) * (ATTN_HEAD_DIM ** -0.5)
    p = jax.nn.softmax(s.astype(jnp.float32), axis=-1).astype(v.dtype)
    return jnp.einsum('bkgqs,bskd->bqkgd', p, v)

def attention_mixer(h, w_in, q_norm, k_norm, w_out, ang_row, ang_col):
    B, L, _ = h.shape
    proj = h @ w_in
    q, k, v, gate = jnp.split(
        proj, [ATTN_WIDTH, ATTN_WIDTH + ATTN_KV_WIDTH, ATTN_WIDTH + 2 * ATTN_KV_WIDTH], axis=-1)
    q = q.reshape(B, L, ATTN_HEADS, ATTN_HEAD_DIM)
    k = k.reshape(B, L, ATTN_KV_HEADS, ATTN_HEAD_DIM)
    v = v.reshape(B, L, ATTN_KV_HEADS, ATTN_HEAD_DIM)
    q = apply_axial_rope(rmsnorm_2(q, q_norm), ang_row, ang_col)
    k = apply_axial_rope(rmsnorm_2(k, k_norm), ang_row, ang_col)
    q = q.reshape(B, L, ATTN_KV_HEADS, ATTN_GROUP, ATTN_HEAD_DIM)
    o_meta = _attend(q[:, :N_META], k, v)
    n_real = L - N_META
    nb = n_real // Q_BLOCK
    q_blocks = q[:, N_META:].reshape(B, nb, Q_BLOCK, ATTN_KV_HEADS, ATTN_GROUP, ATTN_HEAD_DIM)
    o_real = lax.map(lambda qb: _attend(qb, k, v), jnp.swapaxes(q_blocks, 0, 1))
    o_real = jnp.swapaxes(o_real, 0, 1).reshape(B, n_real, ATTN_KV_HEADS, ATTN_GROUP, ATTN_HEAD_DIM)
    o = jnp.concatenate([o_meta, o_real], axis=1).reshape(B, L, ATTN_WIDTH)
    return (o * jax.nn.silu(gate)) @ w_out

def gla_chunked(q, k, v, g, strict):
    B, H, T, dk = q.shape
    dv = v.shape[-1]
    n = T // GLA_CHUNK

    def chunks(t):
        return t.reshape(B, H, n, GLA_CHUNK, t.shape[-1]).astype(jnp.float32)

    qc, kc, vc, gc = chunks(q), chunks(k), chunks(v), chunks(g)
    b = jnp.cumsum(gc, axis=3)
    b_last = b[:, :, :, -1:, :]
    q_dec = qc * jnp.exp(b)
    k_inv = kc * jnp.exp(-b)
    k_end = kc * jnp.exp(b_last - b)
    scores = jnp.einsum('bhncd,bhnsd->bhncs', q_dec, k_inv)
    mask = jnp.tril(jnp.ones((GLA_CHUNK, GLA_CHUNK), bool), k=-1 if strict else 0)
    o_intra = jnp.einsum('bhncs,bhnse->bhnce', jnp.where(mask, scores, 0.0), vc)

    def step(S, xs):
        q_t, k_t, v_t, dl = xs
        o = jnp.einsum('bhcd,bhde->bhce', q_t, S)
        S = S * dl[..., None] + jnp.einsum('bhcd,bhce->bhde', k_t, v_t)
        return S, o

    xs = (jnp.moveaxis(q_dec, 2, 0), jnp.moveaxis(k_end, 2, 0), jnp.moveaxis(vc, 2, 0),
          jnp.moveaxis(jnp.exp(b_last[:, :, :, 0, :]), 2, 0))
    S0 = jnp.zeros((B, H, dk, dv), jnp.float32)
    _, o_inter = lax.scan(step, S0, xs)
    o = o_intra + jnp.moveaxis(o_inter, 0, 2)
    return o.reshape(B, H, T, dv).astype(q.dtype)

def gla_mixer(h, w_in, gk_up, gk_bias, o_norm, w_out):
    B, L, _ = h.shape
    pad = GLA_CHUNK - N_META
    hp = jnp.pad(h, ((0, 0), (pad, 0), (0, 0)))
    T = L + pad
    proj = hp @ w_in
    s1 = GLA_KEY_DIM
    s2 = s1 + GLA_KEY_DIM
    s3 = s2 + GLA_VALUE_DIM
    s4 = s3 + GLA_VALUE_DIM
    s5 = s4 + GLA_GATE_RANK
    q, k, v, g_out, lr_f, lr_b = jnp.split(proj, [s1, s2, s3, s4, s5], axis=-1)

    def heads(t, d):
        return t.reshape(B, T, GLA_HEADS, d).transpose(0, 2, 1, 3)

    def log_gate(lr, up, bias):
        z = (lr @ up + bias).astype(jnp.float32)
        return heads(jax.nn.log_sigmoid(z) / GLA_GATE_NORMALIZER, GLA_HEAD_K)

    q = heads(q, GLA_HEAD_K) * (GLA_HEAD_K ** -0.5)
    k = heads(k, GLA_HEAD_K)
    v = heads(v, GLA_HEAD_V)
    flip = lambda t: jnp.flip(t, axis=2)
    o_f = gla_chunked(q, k, v, log_gate(lr_f, gk_up[0], gk_bias[0]), strict=False)
    o_b = flip(gla_chunked(flip(q), flip(k), flip(v),
                           flip(log_gate(lr_b, gk_up[1], gk_bias[1])), strict=True))
    o = (o_f + o_b).transpose(0, 2, 1, 3)[:, pad:]
    o = rmsnorm_2(o, o_norm).reshape(B, L, GLA_VALUE_DIM)
    return (o * jax.nn.silu(g_out[:, pad:])) @ w_out

def second_inputs(seed: int = 0) -> dict:
    key = jax.random.key(seed)
    ks = jax.random.split(key, 13)
    f32 = jnp.float32
    nrm = lambda k, shape, scale: jax.random.normal(k, shape, f32) * scale
    return {
        "x": nrm(ks[0], (BATCH, SEQ, D_MODEL), 1.0),
        "meta_tokens": nrm(ks[1], (N_META, D_MODEL), 1.0),
        "pre_norm": 1.0 + nrm(ks[2], (DEPTH_2, D_MODEL), 0.02),
        "post_norm": 1.0 + nrm(ks[3], (DEPTH_2, D_MODEL), 0.02),
        "attn_w_in": nrm(ks[4], (N_ATTN_LAYERS, D_MODEL, ATTN_IN), D_MODEL ** -0.5),
        "attn_q_norm": 1.0 + nrm(ks[5], (N_ATTN_LAYERS, ATTN_HEAD_DIM), 0.02),
        "attn_k_norm": 1.0 + nrm(ks[6], (N_ATTN_LAYERS, ATTN_HEAD_DIM), 0.02),
        "attn_w_out": nrm(ks[7], (N_ATTN_LAYERS, ATTN_WIDTH, D_MODEL), ATTN_WIDTH ** -0.5),
        "gla_w_in": nrm(ks[8], (N_GLA_LAYERS, D_MODEL, GLA_IN), D_MODEL ** -0.5),
        "gla_gk_up": nrm(ks[9], (N_GLA_LAYERS, 2, GLA_GATE_RANK, GLA_KEY_DIM), GLA_GATE_RANK ** -0.5),
        "gla_gk_bias": nrm(ks[10], (N_GLA_LAYERS, 2, GLA_KEY_DIM), 0.1),
        "gla_o_norm": 1.0 + nrm(ks[11], (N_GLA_LAYERS, GLA_HEAD_V), 0.02),
        "gla_w_out": nrm(ks[12], (N_GLA_LAYERS, GLA_VALUE_DIM, D_MODEL), GLA_VALUE_DIM ** -0.5),
    }

def second_block(x, meta_tokens, pre_norm, post_norm, attn_w_in, attn_q_norm, attn_k_norm,
              attn_w_out, gla_w_in, gla_gk_up, gla_gk_bias, gla_o_norm, gla_w_out):
    B, S, D = x.shape
    meta = jnp.broadcast_to(meta_tokens.astype(x.dtype)[None], (B, N_META, D))
    h = jnp.concatenate([meta, x], axis=1)
    ang_row, ang_col = axial_rope_angles(S)
    for i in range(DEPTH_2):
        y = rmsnorm_2(h, pre_norm[i])
        j = i // N_MIXERS
        if i % N_MIXERS == 0:
            y = attention_mixer(y, attn_w_in[j], attn_q_norm[j], attn_k_norm[j], attn_w_out[j],
                                ang_row, ang_col)
        else:
            y = gla_mixer(y, gla_w_in[j], gla_gk_up[j], gla_gk_bias[j], gla_o_norm[j], gla_w_out[j])
        h = h + rmsnorm_2(y, post_norm[i])
    return h[:, N_META:]


def setup_inputs(seed=0):
    out = dict(first_inputs(seed))
    for name, value in second_inputs(seed + 1).items():
        if name != "x":
            out[name + "_2"] = value
    return out


def reference(
    x, c, positions, w_ada, b_ada, g_pre_mix, g_post_mix, g_pre_ffn, g_post_ffn, w_in,
    attn_sinks, w_attn_proj, hg_lower_bounds, hg_norm, w_hgrn_proj, w_out, w_ffn_in, w_ffn_out,
    meta_tokens_2, pre_norm_2, post_norm_2, attn_w_in_2, attn_q_norm_2, attn_k_norm_2,
    attn_w_out_2, gla_w_in_2, gla_gk_up_2, gla_gk_bias_2, gla_o_norm_2, gla_w_out_2,
):
    x = first_block(
        x, c, positions, w_ada, b_ada, g_pre_mix, g_post_mix, g_pre_ffn, g_post_ffn, w_in,
        attn_sinks, w_attn_proj, hg_lower_bounds, hg_norm, w_hgrn_proj, w_out, w_ffn_in,
        w_ffn_out,
    )
    return second_block(
        x, meta_tokens_2, pre_norm_2, post_norm_2, attn_w_in_2, attn_q_norm_2, attn_k_norm_2,
        attn_w_out_2, gla_w_in_2, gla_gk_up_2, gla_gk_bias_2, gla_o_norm_2, gla_w_out_2,
    )


_drawn_inputs = setup_inputs


def setup_inputs(seed=0):
    import zlib

    import numpy as np

    out = dict(_drawn_inputs(seed))
    spreads = {}
    factors = {'hg_lower_bounds': 2.785,
     'attn_q_norm_2': 8.0,
     'attn_k_norm_2': 8.0,
     'gla_o_norm_2': 26.086,
     'post_norm_2': 2.746}
    for name, (base, spread) in spreads.items():
        noise = np.random.default_rng([zlib.crc32(name.encode()), seed]).standard_normal(out[name].shape)
        drawn = base * np.exp(spread * noise) if base else spread * noise
        out[name] = __import__('jax').numpy.asarray(drawn.astype(out[name].dtype))
    for name, factor in factors.items():
        out[name] = (out[name] * factor).astype(out[name].dtype)
    return out
```

```python
import numpy as np
from contextlib import ExitStack

import concourse.bass as bass
from concourse import mybir

F32, F32R, I32, U32 = mybir.dt.float32, mybir.dt.float32r, mybir.dt.int32, mybir.dt.uint32
ACT, ALU, AX = mybir.ActivationFunctionType, mybir.AluOpType, mybir.AxisListType

P = 128
D = 2048
KT = D // P
S = 256
META = 16
T2 = S + META
EPS = 1e-6
SLOTS = 4
UNIT = KT * 256
SUB = UNIT // 8
FFN = 5632
CH = 64
NCH = S // CH
HG = 8


class Counter:

    def __init__(self, sem):
        self.sem, self.count = sem, 0


class Token:

    def __init__(self, counter, value, loop):
        self.counter, self.value, self.loop = counter, value, loop


class Loop:
    def __init__(self, n, steps, before, after):
        self.n, self.steps, self.before, self.after = n, steps, before, after


class Program:

    def __init__(self, nc, ctx):
        self.nc, self.ctx, self.counters = nc, ctx, []
        self.writing, self.loop, self.it, self.events = True, None, 0, {}
        self.always = self.counter("consts_in")
        self.pe, self.act, self.dve, self.pool, self.sp = (
            Engine(self, e, n) for e, n in ((nc.tensor, "pe_done"), (nc.scalar, "act_done"),
                                            (nc.vector, "dve_done"), (nc.gpsimd, "pool_done"), (nc.sync, "sp_done")))

    def counter(self, name):
        self.counters.append(Counter(self.ctx.enter_context(self.nc.semaphore(name))))
        return self.counters[-1]

    def note(self, event, *tokens):
        self.events[event] = list(tokens)

    def upcoming(self, counter, add):
        return Token(counter, counter.count + add, self.loop)

    def value(self, token):
        if token.loop is None:
            return 0, token.value
        step = token.loop.steps.get(token.counter, 0)
        if token.loop is self.loop:
            return step, token.value
        return 0, token.value + (token.loop.n - 1) * step

    def last(self, event):
        now = self.events.get(event, [])
        if self.loop is None or (now and now[0].loop is self.loop):
            return [(t.counter, *self.value(t)) for t in now]
        out = {t.counter: (0, self.value(t)[1]) for t in now}
        for t in self.loop.after.get(event, []):
            if t.loop == "counting":
                step = self.loop.steps[t.counter]
                assert t.value - step > 0, (event, t.value, step)
                out[t.counter] = (step, max(t.value - step, out.get(t.counter, (0, 1))[1]))
        return [(c, m, v) for c, (m, v) in out.items()]

    def repeat(self, n, body):
        start = {c: c.count for c in self.counters}
        before = dict(self.events)
        self.writing, self.loop, seen = False, Loop(n, {}, before, {}), self.loop
        marks = self.loop
        body(0)
        steps = {c: c.count - start[c] for c in self.counters if c.count > start[c]}
        after = {k: [Token(t.counter, t.value, "counting") for t in v] for k, v in self.events.items()
                 if v and v[0].loop is marks}
        for c, v in start.items():
            c.count = v
        self.events = before
        self.writing, self.loop = True, Loop(n, steps, before, after)
        for e in (self.pe, self.act, self.dve, self.pool, self.sp):
            e.seen = {}
        with self.nc.Fori(0, n) as it:
            self.it = it
            body(it)
        for c, step in steps.items():
            assert c.count == start[c] + step
            c.count = start[c] + n * step
        self.loop, self.it = None, 0
        for e in (self.pe, self.act, self.dve, self.pool, self.sp):
            e.seen = {}


class Engine:
    def __init__(self, program, engine, name):
        self.p, self.e, self.seen = program, engine, {}
        self.settle = name in ("act_done", "sp_done")
        self.done = program.counter(name)

    def wait(self, *what):
        waits = []
        for w in what:
            if w is not None:
                waits += self.p.last(w) if isinstance(w, str) else [(w.counter, *self.p.value(w))]
        most = {}
        for c, mult, const in waits:
            most[(c, mult)] = max(const, most.get((c, mult), 0))
        waits = [(c, mult, const) for (c, mult), const in most.items() if self.seen.get((c, mult), 0) < const]
        for c, mult, const in waits:
            self.seen[(c, mult)] = max(const, self.seen.get((c, mult), 0))
        if not self.p.writing:
            return
        waits = [(c, self.e.to_reg(self.p.it * mult + const) if mult and self.settle else
                  self.p.it * mult + const if mult else const, mult) for c, mult, const in waits]
        if self.settle and any(mult for _, _, mult in waits):
            self.e.wait_ge(self.p.always.sem, 16)
        for c, value, _ in waits:
            self.e.wait_ge(c.sem, value)

    def do(self, write, *after, counter=None, add=1):
        self.wait(*after)
        c = counter or self.done
        if self.p.writing:
            write(self.e).then_inc(c.sem, add)
        c.count += add
        return Token(c, c.count, self.p.loop)


ROT1, ROT2 = 16, 64


def const_tables():
    t = {"ident": np.eye(P, dtype=np.float32), "ones": np.ones((P, P), np.float32)}
    p = np.arange(P)
    rot = np.zeros((P, P), np.float32)
    for h in (0, 64):
        for j in range(8):
            rot[h + 8 + j, h + j] = -1.0
            rot[h + j, h + 8 + j] = 1.0
    t["rot1"] = rot
    inv = (np.float32(500000.0) ** (-np.arange(0, ROT1, 2, dtype=np.float32) / np.float32(ROT1))).astype(np.float32)
    freq = np.zeros((P, 1), np.float32)
    for q in range(P):
        if q % 64 < ROT1:
            freq[q, 0] = inv[q % 8]
    t["freq1"] = freq
    rot = np.zeros((P, P), np.float32)
    for h in (0, 64):
        for j in range(32):
            rot[h + 32 + j, h + j] = -1.0
            rot[h + j, h + 32 + j] = 1.0
    t["rot2"] = rot
    inv = (np.float32(10000.0) ** (-np.arange(0, ROT2, 2, dtype=np.float32) / np.float32(ROT2))).astype(np.float32)
    pos = np.arange(S)
    ang = np.zeros((P, T2), np.float32)
    for q in range(P):
        axis = (pos // 64 if q < 64 else pos % 64).astype(np.float32)
        ang[q, :S] = axis * inv[q % 32]
    t["cos2"], t["sin2"] = np.cos(ang).astype(np.float32), np.sin(ang).astype(np.float32)
    qi, kj = np.arange(P)[:, None], np.arange(P)[None, :]
    t["prev"] = np.where(kj > qi, 0.0, -1e30).astype(np.float32)
    t["own"] = np.where(kj <= qi, 0.0, -1e30).astype(np.float32)
    s, u = (p % CH)[:, None], np.arange(CH)[None, :]
    t["diag"] = (s == u).astype(np.float32)
    for m in (32, 16, 8, 4, 2, 1):
        same = (s // (2 * m)) == (u // (2 * m))
        t[f"lvl{m}"] = (same & (s % (2 * m) < m) & (u % (2 * m) >= m)).astype(np.float32)
    t["later"] = (s > u).astype(np.float32)
    at, cols, n = {}, [], 0
    for k, v in t.items():
        at[k] = (n, n + v.shape[1])
        cols.append(v)
        n += v.shape[1]
    return at, np.concatenate(cols, axis=1)


def flat(ap):
    return ap.rearrange("p a b -> p (a b)")


def build(nc, x, c, positions, w_ada, b_ada, g_pre_mix, g_post_mix, g_pre_ffn, g_post_ffn, w_in, attn_sinks,
          w_attn_proj, hg_lower_bounds, hg_norm, w_hgrn_proj, w_out, w_ffn_in, w_ffn_out, meta_tokens_2,
          pre_norm_2, post_norm_2, attn_w_in_2, attn_q_norm_2, attn_k_norm_2, attn_w_out_2, gla_w_in_2,
          gla_gk_up_2, gla_gk_bias_2, gla_o_norm_2, gla_w_out_2, consts, out):
    ctx = ExitStack()
    with ctx:
        k = Kernel(nc, ctx, consts)
        k.gla_w_in, k.gla_up = gla_w_in_2[0], gla_gk_up_2[0]
        k.start(x, c, positions, meta_tokens_2, attn_sinks,
                [[(c, 16), (g_pre_mix, 16), (g_post_mix, 16), (g_pre_ffn, 16), (g_post_ffn, 16),
                  (hg_lower_bounds, 16), (pre_norm_2, 32)],
                 [(post_norm_2, 32), (gla_gk_bias_2, 16), (gla_o_norm_2, 4), (attn_q_norm_2, 1),
                  (attn_k_norm_2, 1), (hg_norm, 1)],
                 [(b_ada, 96)]])
        k.first_block(w_ada[0], w_in[0], w_attn_proj[0], w_hgrn_proj[0], w_out[0], w_ffn_in[0], w_ffn_out[0])
        k.second_block(attn_w_in_2[0], attn_w_out_2[0], gla_w_in_2[0], gla_w_out_2[0])
        k.finish(out)


def columns(w, c0, k0=0, kt=KT, n=256):
    return w[k0 * P:(k0 + kt) * P, bass.ds(c0, n)].rearrange("(k p) n -> p k n", p=P)


class Kernel:
    def __init__(self, nc, ctx, consts):
        self.nc, self.consts = nc, consts
        p = self.p = Program(nc, ctx)
        self.pe, self.act, self.dve, self.pool, self.sp = p.pe, p.act, p.dve, p.pool, p.sp
        self.top = 1152

        def sb(name, shape, dtype=F32, at=None):
            n = 4 * int(np.prod(shape[1:]))
            n += -n % 32
            if at is None:
                at, self.top = self.top, self.top + n
            assert at + n <= 229344, (name, at, n)
            return nc.alloc_sbuf_tensor_at(name, shape, dtype, offset=at)

        self.sb = sb
        self.raw = sb("raw", [P, SLOTS, UNIT])
        self.split_at = self.top
        self.wh = sb("wh", [P, 4, SUB], F32R)
        self.wl = sb("wl", [P, 4, SUB], F32R)
        self.X = sb("X", [P, KT, T2])
        self.ah_at = self.top
        self.ah = sb("ah", [P, KT, T2], F32R)
        self.al = sb("al", [P, KT, T2], F32R)
        self.cat, table = const_tables()
        self.nconst = table.shape[1]
        self.cs = sb("cs", [P, self.nconst])
        self.vec = sb("vec", [P, 3, P])
        self.mod = sb("mod", [P, 96])
        self.sinks = sb("sinks", [P, 16])
        self.col = sb("col", [P, 8])
        self.scale1 = sb("scale1", [P, KT])
        self.gate1 = sb("gate1", [P, KT])
        self.work = self.top
        self.acc = sb("acc", [P, 2, 2, 256])
        self.sq = sb("sq", [P, 4, T2])
        self.tmp_at = self.top
        self.tmp, self.tmp2 = sb("tmp", [P, 2, T2]), sb("tmp2", [P, 2, T2])
        self.rs, self.rs2 = sb("rs", [P, T2]), sb("rs2", [P, T2])
        self.big = self.top
        self.bank = ctx.enter_context(nc.psum_tensor("bank", [P, 8, 512], F32))
        self.arrived = [p.counter(f"raw{i}_arrived") for i in range(SLOTS)]
        self.high = p.counter("wh_made")
        self.low = p.counter("wl_made")
        self.used = p.counter("eighth_multiplied")
        self.ada_sum = p.counter("ada_unit_summed")
        self.small_in = p.counter("small_loads")
        self.stored = p.counter("stored")
        self.units = 0
        self.sq_turn = 0

    def C(self, name, a=None, b=None):
        lo, hi = self.cat[name]
        lo, hi = (lo, hi) if a is None else (lo + a, lo + b)
        return self.cs[:, lo:hi]

    def load(self, first, second):
        slot = self.units % SLOTS
        self.units += 1
        self.sp.wait(f"raw{slot} read")
        for where, view in (first, second):
            dst = where(self.raw[:, slot, :])
            self.sp.do(lambda e, dst=dst, view=view: e.dma_start(dst, view), counter=self.arrived[slot], add=16)
        return slot

    def load_columns(self, w, c0, k0=0):
        half = lambda i: (lambda r: r.rearrange("p (k n) -> p k n", n=256)[:, 8 * i:8 * i + 8, :],
                          columns(w, c0, k0 + 8 * i, 8))
        return self.load(half(0), half(1))

    def landed(self, slot, pending=False):
        c = self.arrived[slot]
        return self.p.upcoming(c, 32) if pending else Token(c, c.count, self.p.loop)

    def split(self, slot, q, landed):
        src, r = self.raw[:, slot, q * SUB:(q + 1) * SUB], q % 4
        high = self.act.do(lambda e: e.activation(self.wh[:, r, :], src, ACT.Copy),
                           landed, f"w{r} used", counter=self.high)
        low = self.dve.do(lambda e: e.tensor_tensor(self.wl[:, r, :], src, self.wh[:, r, :].bitcast(F32),
                                                    ALU.subtract), high, counter=self.low)
        if q == 7:
            self.p.note(f"raw{slot} read", low)
        self.p.note(f"w{r} split", low)

    def split_first(self):
        for q in range(4):
            self.split(self.units % SLOTS, q, self.landed(self.units % SLOTS, pending=True))

    def unit(self, slot, plan, nxt=None, pending=False, free=(), ready=(), between=None):
        here = self.landed(slot)
        there = None if nxt is None else self.landed(nxt, pending)
        self.pe.wait(*free)
        for q in range(8):
            self.pe.wait(*ready[q:q + 1])

            def products(e, q=q):
                for dst, cols, ah, al, start, stop in plan[q]:
                    wh, wl = cols(self.wh[:, q % 4, :]), cols(self.wl[:, q % 4, :])
                    e.matmul(dst, wh, ah, start=start, stop=False, skip_group_check=True)
                    e.matmul(dst, wh, al, start=False, stop=False, skip_group_check=True)
                    last = e.matmul(dst, wl, ah, start=False, stop=stop, skip_group_check=True)
                return last
            done = self.pe.do(products, f"w{q % 4} split", counter=self.used)
            self.p.note(f"w{q % 4} used", done)
            if between:
                between(q)
            if q < 4:
                self.split(slot, q + 4, here)
            elif nxt is not None:
                self.split(nxt, q - 4, there)
        return done

    def plan(self, outs, T, k0=0, ah=None, al=None):
        ah, al = ah or self.ah, al or self.al

        def cols(kk, j):
            return lambda w: w[:, kk * 256 + j * P:kk * 256 + (j + 1) * P]
        return [[(outs[j], cols(kk, j), ah[:, 2 * q + kk, 0:T], al[:, 2 * q + kk, 0:T],
                  q == 0 and kk == 0, q == 7 and kk == 1) for j in range(2) for kk in range(2)] for q in range(8)]

    def b(self, i, n=T2, lo=0, p=P, p0=0):
        return self.bank[p0:p0 + p, i, lo:lo + n]

    def ada_step(self, slot, turn, q, n=2):
        if q == 0:
            self.dve.wait(self.landed(slot), f"acc{turn} read")
        for kk in range(n * q, n * q + n):
            acc = self.acc[:, turn, kk % 2, :]
            w, ccol = self.raw[:, slot, kk * 256:(kk + 1) * 256], self.vec[:, 0, kk:kk + 1]
            last = dict(counter=self.ada_sum) if kk == KT - 1 else {}
            if kk < 2:
                t = self.dve.do(lambda e: e.tensor_scalar(acc, w, ccol, None, ALU.mult))
            else:
                t = self.dve.do(lambda e: e.scalar_tensor_tensor(out=acc, in0=w, scalar=ccol, in1=acc, op0=ALU.mult,
                                                                 op1=ALU.add), f"chain{kk % 2}", **last)
            self.p.note(f"chain{kk % 2}", t)
            if kk == KT - 2:
                self.even_done = t
            if kk == KT - 1:
                self.p.note(f"raw{slot} read", t)
                self.p.note(f"acc{turn} made", self.even_done, t)

    def ada_columns(self, turn, index):
        def sums(e):
            for j in range(2):
                for ch in range(2):
                    last = e.matmul(self.bank[:, 7, bass.ds(index * 2 + j, 1)], self.acc[:, turn, ch, j * P:(j + 1) * P],
                                    self.C("ones", 0, 1), start=ch == 0, stop=ch == 1, skip_group_check=True)
            return last
        self.p.note(f"acc{turn} read", self.pe.do(sums, f"acc{turn} made", "bank7 read"))

    def ada_take(self, lo, hi):
        t = self.dve.do(lambda e: e.tensor_tensor(self.mod[:, lo:hi], self.bank[:, 7, lo:hi], self.vec[:, 2, lo:hi],
                                                  ALU.add), "acc0 read", "acc1 read")
        self.p.note("bank7 read", t)
        return t

    def rstd(self, bank, n, width, tile, summed):
        root = self.act.do(lambda e: e.activation(tile, self.b(bank, n), ACT.Sqrt, bias=self.col[:, 0:1],
                                                  scale=1.0 / width), summed)
        self.p.note(f"bank{bank} read", root)
        return self.dve.do(lambda e: e.reciprocal(tile, tile), root)

    def square_into(self, src, n, first, last, after, engine=None):
        t = self.sq_turn = (self.sq_turn + 1) % 4
        sq = self.sq[:, t, 0:n]
        a = self.act.do(lambda e: e.activation(sq, src, ACT.Square), after, f"sq{t} read")
        m = self.pe.do(lambda e: e.matmul(self.b(6, n), self.C("ones"), sq, start=first, stop=last,
                                          skip_group_check=True), a, *(["bank6 read"] if first else []))
        self.p.note(f"sq{t} read", m)
        return m

    def operand_tile(self, kt, n, rs, rs_ready, scale, shift, after):
        t = kt % 2
        tmp = self.tmp[:, t, 0:n]
        a = self.pool.do(lambda e: e.tensor_tensor(tmp, self.X[:, kt, 0:n], rs, ALU.mult),
                         rs_ready, after, f"tmp{t} read")
        full = self.tmp2[:, t, 0:n]
        if shift is None:
            f = self.dve.do(lambda e: e.tensor_scalar(full, tmp, scale, None, ALU.mult), a, f"full{t} read")
        else:
            f = self.dve.do(lambda e: e.tensor_scalar(full, tmp, scale, shift, ALU.mult, ALU.add), a, f"full{t} read")
        self.p.note(f"tmp{t} read", f)
        h = self.act.do(lambda e: e.activation(self.ah[:, kt, 0:n], full, ACT.Copy), f)
        l = self.dve.do(lambda e: e.tensor_tensor(self.al[:, kt, 0:n], full, self.ah[:, kt, 0:n].bitcast(F32),
                                                  ALU.subtract), h)
        self.p.note(f"full{t} read", l)
        return l

    def operand(self, n, rs, scale, shift, rs_ready, after=None):
        self.act.wait("operand free")
        self.dve.wait("operand free")
        for kt in range(KT):
            t = self.operand_tile(kt, n, rs[:, 0:n], rs_ready, scale[:, kt:kt + 1],
                                  None if shift is None else shift[:, kt:kt + 1], after)
            if kt % 2:
                self.p.note(f"operand {kt // 2}", t)

    READY = [f"operand {q}" for q in range(8)]

    def residual(self, n, m_n, y, y_ready, coef, post_summed):
        r = self.rstd(6, n, D, self.rs[:, 0:n], post_summed)
        for kt in range(KT):
            t = kt % 2
            tmp = self.tmp[:, t, 0:n]
            a = self.pool.do(lambda e: e.tensor_tensor(tmp, y[:, kt, 0:n], self.rs[:, 0:n], ALU.mult), r, y_ready,
                             f"tmp{t} read")
            f = self.dve.do(lambda e: e.scalar_tensor_tensor(out=self.X[:, kt, 0:n], in0=tmp, scalar=coef[:, kt:kt + 1],
                                                             in1=self.X[:, kt, 0:n], op0=ALU.mult, op1=ALU.add), a)
            self.p.note(f"tmp{t} read", f)
            m = self.square_into(self.X[:, kt, 0:m_n], m_n, kt == 0, kt == KT - 1, f)
        self.x_done = f
        return self.rstd(6, m_n, D, self.rs2[:, 0:m_n], m)

    def join(self):
        engines = (self.pe, self.act, self.dve, self.pool)
        now = [Token(e.done, e.done.count, None) for e in engines if e.done.count]
        now += [Token(c, c.count, None) for c in (self.used,) if c.count]
        for e in engines:
            e.wait(*now)
        return now

    def start(self, x, c, positions, meta, sinks, groups):
        sp, p = self.sp, self.p
        consts_in, rows_in, x_in = p.always, p.counter("rows_in"), p.counter("x_in")
        self.rows = self.sb("rows", [P, 3, P], at=self.big)
        self.xrows = self.sb("xrows", [P, 2, D], at=self.big + 1536)
        self.mrows = self.sb("mrows", [META, D], at=self.big + 1536 + 16384)
        self.pos = self.sb("pos", [P, S], I32, at=self.big + 44000)
        self.angle = self.sb("angle", [P, 2, S], at=self.big + 45024)

        sp.do(lambda e: e.dma_start(self.cs[:, :], self.consts), counter=consts_in, add=16)
        for g, group in enumerate(groups):
            at = 0
            for ap, n in group:
                dims = " ".join("abc"[:len(ap.shape) - 1])
                view = ap.rearrange(f"{dims} (j p) -> ({dims} j) p", p=P) if len(ap.shape) > 1 else ap
                sp.do(lambda e, view=view, at=at, n=n, g=g: e.dma_start(self.rows[at:at + n, g, :], view),
                      counter=rows_in, add=16)
                at += n
        sp.do(lambda e: e.dma_start(self.xrows[:, :, :], x[0].rearrange("(i p) d -> p i d", p=P)), counter=x_in, add=16)
        sp.do(lambda e: e.dma_start(self.mrows[:, :], meta), counter=x_in, add=16)
        sp.do(lambda e: e.dma_start(self.pos[:, :], positions.to_broadcast([P, S])), counter=x_in, add=16)
        sp.do(lambda e: e.dma_start(self.sinks[:, :], sinks.to_broadcast([P, 16])), counter=x_in, add=16)
        consts, rows, xs = (Token(q, q.count, None) for q in (consts_in, rows_in, x_in))
        self.dve.do(lambda e: e.memset(self.col[:, 0:1], EPS))
        cols = self.dve.do(lambda e: e.memset(self.col[:, 1:2], 1.0))
        self.pool.wait(cols)
        self.act.wait(cols)
        for e in (self.pe, self.act, self.dve, self.pool):
            e.wait(consts, rows, xs)

        def vec_rows(e):
            for g, n in enumerate((128, 55, 96)):
                last = e.transpose(self.b(0, n, g * P), self.rows[0:n, g, :], self.cs[0:n, self.cat["ident"][0]:
                                                                                self.cat["ident"][0] + n])
            return last
        t = self.pe.do(vec_rows)
        for g, n in enumerate((128, 55, 96)):
            self.vec_done = self.act.do(lambda e: e.activation(self.vec[:, g, 0:n], self.b(0, n, g * P), ACT.Copy), t)
        p.note("bank0 read", self.vec_done)
        self.dve.wait(self.vec_done)
        self.pe.wait(self.vec_done)
        for n, (i, g) in enumerate((i, g) for i in range(2) for g in range(4)):
            bank = 1 + n % 4

            def turn(e):
                for j in range(4):
                    last = e.transpose(self.b(bank, P, j * P), self.xrows[:, i, (4 * g + j) * P:(4 * g + j + 1) * P],
                                       self.C("ident"))
                return last
            t = self.pe.do(turn, f"bank{bank} read")
            t = self.act.do(lambda e: e.activation(self.X[:, 4 * g:4 * g + 4, i * P:(i + 1) * P],
                                                   self.b(bank, 512).rearrange("p (k n) -> p k n", k=4), ACT.Copy), t)
            p.note(f"bank{bank} read", t)

        def turn_meta(e):
            for j in range(KT):
                last = e.transpose(self.b(5, META, j * META), self.mrows[:, j * P:(j + 1) * P],
                                   self.cs[0:META, self.cat["ident"][0]:self.cat["ident"][0] + META])
            return last
        t = self.pe.do(turn_meta)
        t = self.x_done = self.act.do(lambda e: e.activation(
            self.X[:, :, S:T2], self.b(5, 256).rearrange("p (k n) -> p k n", k=KT), ACT.Copy), t)
        self.wlr = self.sb("wlr", [P, KT, 32], at=self.big + 57344)
        self.up = self.sb("up", [32, 2, 1024], at=self.big + 57344 + 2048)
        self.low_in = p.counter("low_rank_in")
        z = self.pool.do(lambda e: e.memset(self.up[:, :, :], 0.0))
        sp.do(lambda e: e.dma_start(self.wlr[:, :, :], columns(self.gla_w_in, 6144, n=32)), counter=self.low_in, add=16)
        for d in range(2):
            sp.do(lambda e: e.dma_start(self.up[16 * d:16 * d + 16, d, :], self.gla_up[d]), z, counter=self.low_in,
                  add=16)
        ang, turns = self.angle[:, 0, :], self.angle[:, 1, :]
        self.cos1, self.sin1 = self.angle[:, 0, :], self.angle[:, 1, :]
        two_pi = 2 * np.pi
        c1 = 6.28125
        c2 = float(np.float32(two_pi - c1).view(np.uint32) & np.uint32(0xFFFFF000))
        c2 = float(np.array(int(c2), np.uint32).view(np.float32))
        c3 = two_pi - c1 - c2
        dve = self.dve
        t = dve.do(lambda e: e.tensor_copy(ang, self.pos[:, :]), t)
        t = dve.do(lambda e: e.tensor_scalar(ang, ang, self.C("freq1"), None, ALU.mult), t)
        t = dve.do(lambda e: e.tensor_scalar(turns, ang, float(1 / two_pi), 12582912.0, ALU.mult, ALU.add), t)
        t = dve.do(lambda e: e.tensor_scalar(turns, turns, 12582912.0, None, ALU.subtract), t)
        for part in (c1, c2, c3):
            t = dve.do(lambda e: e.scalar_tensor_tensor(out=ang, in0=turns, scalar=-float(part), in1=ang, op0=ALU.mult,
                                                        op1=ALU.add), t)
        t = dve.do(lambda e: e.tensor_scalar(ang, ang, 3.1415925, -3.1415925, ALU.min, ALU.max), t)
        t = self.act.do(lambda e: e.activation(self.sin1, ang, ACT.Sin), t)
        t = self.act.do(lambda e: e.activation(self.cos1, ang, ACT.Sin, scale=0.5), t)
        t = dve.do(lambda e: e.tensor_tensor(self.cos1, self.cos1, self.cos1, ALU.mult), t)
        self.trig = dve.do(lambda e: e.tensor_scalar(self.cos1, self.cos1, -2.0, 1.0, ALU.mult, ALU.add), t)

    def first_block(self, w_ada, w_in, w_ap, w_hp, w_out, w_fi, w_fo):
        p, pe, act, dve = self.p, self.pe, self.act, self.dve
        cols = lambda g, n=16: self.vec[:, 0, g:g + n]
        self.dve.do(lambda e: e.memset(self.acc[:, :, :, :], 0.0), counter=self.ada_sum, add=4)
        self.pe.do(lambda e: e.matmul(self.b(7, 4), self.C("ones"), self.C("ones", 0, 4), start=True, stop=True),
                   counter=self.used, add=32)
        self.dve.do(lambda e: e.memset(self.col[:, 2:3], 0.0), counter=self.low, add=32)
        self.act.do(lambda e: e.activation(self.col[:, 3:4], self.col[:, 0:1], ACT.Copy), counter=self.high, add=32)

        for kt in range(KT):
            m = self.square_into(self.X[:, kt, 0:S], S, kt == 0, kt == KT - 1, self.x_done)
        rs = self.rstd(6, S, D, self.rs[:, 0:S], m)

        def ada_body(it):
            slots = [self.load_columns(w_ada, (it * 4 + j) * 256) for j in range(4)]
            for j, slot in enumerate(slots):
                for q in range(8):
                    self.ada_step(slot, j % 2, q)
                self.ada_columns(j % 2, it * 4 + j)
        p.repeat(4, ada_body)
        t = self.ada_take(0, 32)
        t = dve.do(lambda e: e.tensor_scalar(self.scale1[:, :], self.mod[:, 16:32], 1.0, None, ALU.add), t)
        t = dve.do(lambda e: e.tensor_tensor(self.scale1[:, :], self.scale1[:, :], cols(16), ALU.mult), t)
        dve.wait(t)
        self.operand(S, self.rs, self.scale1, self.mod[:, 0:16], rs)

        proj = self.proj = self.sb("proj1", [P, 42, S], at=self.big)
        self.join()

        def evict(dst, banks, done, n=S):
            for j in range(2):
                t = act.do(lambda e, j=j: e.activation(dst(j), self.b(banks[j], n), ACT.Copy), done)
                p.note(f"bank{banks[j]} read", t)
            return t

        def w_in_body(it):
            slots = []
            for j in range(2):
                slots.append(self.load_columns(w_in, (it * 2 + j) * 256))
                slots.append(self.load_columns(w_ada, (it * 2 + j + 16) * 256))
            for j in range(2):
                banks = (2 * j, 2 * j + 1)
                done = self.unit(slots[2 * j], self.plan([self.b(i, S) for i in banks], S), slots[(2 * j + 2) % 4],
                                 pending=j == 1, free=[f"bank{i} read" for i in banks], ready=self.READY,
                                 between=lambda q, j=j: self.ada_step(slots[2 * j + 1], j, q))
                evict(lambda i: flat(proj[:, bass.ds((it * 2 + j) * 2 + i, 1), :]), banks, done)
                self.ada_columns(j, it * 2 + j + 16)
        self.split_first()
        p.repeat(10, w_in_body)
        tail = self.load_columns(w_in, 20 * 256)
        merge_first = self.units % SLOTS
        done = self.unit(tail, self.plan([self.b(0, S), self.b(1, S)], S), merge_first, pending=True,
                         free=["bank0 read", "bank1 read"])
        evict(lambda i: proj[:, 40 + i, :], (0, 1), done)
        self.ada_take(32, 72)
        self.join()
        self.attention1()
        self.join()
        self.hgrn()
        self.join()
        self.merge(w_in, w_ap, w_hp, w_ada)
        self.ada_take(72, 88)
        self.join()

        t = dve.do(lambda e: e.tensor_tensor(self.gate1[:, :], self.mod[:, 32:48], cols(32), ALU.mult))
        t = dve.do(lambda e: e.tensor_scalar(self.scale1[:, :], self.mod[:, 64:80], 1.0, None, ALU.add), t)
        t = dve.do(lambda e: e.tensor_tensor(self.scale1[:, :], self.scale1[:, :], cols(48), ALU.mult), t)
        dve.wait(t)
        y = self.y = self.sb("y", [P, KT, T2], at=self.big + 32768)
        summed = self.to_y(w_out, S)
        self.join()
        rs = self.residual(S, S, y, None, self.gate1, summed)
        self.operand(S, self.rs2, self.scale1, self.mod[:, 48:64], rs)
        self.join()

        self.feed_forward(w_fi, w_fo, w_ada)
        self.join()
        t = dve.do(lambda e: e.tensor_tensor(self.gate1[:, :], self.mod[:, 80:96], cols(64), ALU.mult))
        dve.wait(t)
        for kt in range(KT):
            m = self.square_into(y[:, kt, 0:S], S, kt == 0, kt == KT - 1, None)
        rs = self.residual(S, T2, y, None, self.gate1, m)
        self.operand(T2, self.rs2, self.vec[:, 0, 96:112], None, rs)
        self.join()

    def merge(self, w_in, w_ap, w_hp, w_ada):
        p, pe, act, dve, pool, proj = self.p, self.pe, self.act, self.dve, self.pool, self.proj
        at = self.big + 18432
        parts = [self.sb(n, [P, 8, S], F32R, at=at + 8192 * i) for i, n in enumerate(("oah", "oal", "ohh", "ohl"))]
        merged = self.sb("merged", [P, KT, S], at=self.big)
        for i, t0 in enumerate((0, 10)):
            h, l = parts[2 * i], parts[2 * i + 1]
            src = flat(proj[:, t0:t0 + 8, :])
            t = act.do(lambda e: e.activation(flat(h[:, :, :]), src, ACT.Copy))
            t = dve.do(lambda e: e.tensor_tensor(flat(l[:, :, :]), src, flat(h[:, :, :]).bitcast(F32), ALU.subtract), t)
        self.join()

        def body(it):
            col = it * 256
            half = lambda w, i: (lambda r: r.rearrange("p (k n) -> p k n", n=256)[:, 8 * i:8 * i + 8, :],
                                 columns(w, col, 0, 8))
            slots = [self.load_columns(w_in, col + 21 * 256), self.load_columns(w_in, col + 29 * 256),
                     self.load(half(w_ap, 0), half(w_hp, 1)), self.load_columns(w_ada, (it + 36) * 256)]
            for i in range(2):
                sg = (self.tmp, self.tmp2)[i]
                banks = (2 * i, 2 * i + 1)
                done = self.unit(slots[i], self.plan([self.b(j, S) for j in banks], S), slots[i + 1],
                                 free=[f"bank{j} read" for j in banks],
                                 between=lambda q, i=i: self.ada_step(slots[3], 0, q + 8 * i, n=1))
                for j in range(2):
                    t = act.do(lambda e: e.activation(sg[:, j, 0:S], self.b(banks[j], S), ACT.Sigmoid), done,
                               f"sg{i} read")
                    p.note(f"bank{banks[j]} read", t)
                p.note(f"sg{i} made", t)

            def cols(kk, j):
                return lambda w: w[:, kk * 256 + j * P:kk * 256 + (j + 1) * P]
            plan = [[(self.b(4 + j, S, (q // 4) * S), cols(kk, j), parts[2 * (q // 4)][:, 2 * (q % 4) + kk, :],
                      parts[2 * (q // 4) + 1][:, 2 * (q % 4) + kk, :], q % 4 == 0 and kk == 0, q % 4 == 3 and kk == 1)
                     for j in range(2) for kk in range(2)] for q in range(8)]
            done = self.unit(slots[2], plan, slots[0], pending=True, free=["bank4 read", "bank5 read"])
            self.ada_columns(0, it + 36)
            for i in range(2):
                sg = (self.tmp, self.tmp2)[i]
                ps = self.bank[:, 4:6, i * S:(i + 1) * S]
                t = dve.do(lambda e: e.tensor_tensor(sg[:, :, 0:S], sg[:, :, 0:S], ps, ALU.mult), done, f"sg{i} made")
            p.note("bank4 read", t)
            p.note("bank5 read", t)
            t = pool.do(lambda e: e.tensor_tensor(merged[:, bass.ds(it * 2, 2), :], self.tmp[:, :, 0:S],
                                                  self.tmp2[:, :, 0:S], ALU.add), t)
            p.note("sg0 read", t)
            p.note("sg1 read", t)
        p.repeat(8, body)
        self.join()
        for kt in range(KT):
            h = act.do(lambda e: e.activation(self.ah[:, kt, 0:S], merged[:, kt, :], ACT.Copy))
            t = dve.do(lambda e: e.tensor_tensor(self.al[:, kt, 0:S], merged[:, kt, :],
                                                 self.ah[:, kt, 0:S].bitcast(F32), ALU.subtract), h)
            if kt % 2:
                p.note(f"operand {kt // 2}", t)

    def to_y(self, w, n, last=False):
        p, pe, act, dve, y = self.p, self.pe, self.act, self.dve, self.y
        z = dve.do(lambda e: e.memset(self.sq[:, :, :], 0.0), *[f"sq{i} read" for i in range(4)])
        p.note("squares1 made", z)
        pe.do(lambda e: e.matmul(self.b(6, n), self.C("ones"), self.sq[:, 0, 0:n], start=True, stop=False,
                                 skip_group_check=True), z, "bank6 read")

        def add_squares(turn, stop=False):
            def products(e):
                for j in range(2):
                    last = e.matmul(self.b(6, n), self.C("ones"), self.sq[:, 2 * turn + j, 0:n], start=False,
                                    stop=stop and j == 1, skip_group_check=True)
                return last
            t = pe.do(products, f"squares{turn} made")
            p.note(f"squares{turn} read", t)
            return t

        def body(it, end=False):
            slots = [self.load_columns(w, (it * 4 + j) * 256) for j in range(4)]
            for j in range(4):
                turn = j % 2
                banks = (2 * turn, 2 * turn + 1)
                nxt = None if end and j == 3 else slots[(j + 1) % 4]
                done = self.unit(slots[j], self.plan([self.b(i, n) for i in banks], n), nxt, pending=j == 3,
                                 free=[f"bank{i} read" for i in banks], ready=self.READY)
                add_squares(1 - turn)
                for i in range(2):
                    act.do(lambda e: e.activation(flat(y[:, bass.ds((it * 4 + j) * 2 + i, 1), 0:n]),
                                                  self.b(banks[i], n), ACT.Copy), done)
                    t = act.do(lambda e: e.activation(self.sq[:, 2 * turn + i, 0:n], self.b(banks[i], n), ACT.Square),
                               f"squares{turn} read")
                    p.note(f"bank{banks[i]} read", t)
                p.note(f"squares{turn} made", t)
            p.note("operand free", done)
        if last:
            body(0)
            body(1, end=True)
        else:
            p.repeat(2, body)
        t = add_squares(1, stop=True)
        for i in range(4):
            p.note(f"sq{i} read", t)
        return t

    def feed_forward(self, w_fi, w_fo, w_ada):
        p, pe, act, dve, y = self.p, self.pe, self.act, self.dve, self.y
        fh = self.sb("fh", [P, KT, S], F32R, at=self.big)
        fl = self.sb("fl", [P, KT, S], F32R, at=self.big + 16384)

        def hidden_load(tile):
            half = lambda i: (lambda r: r.rearrange("p (k n) -> p k n", n=256)[:, :, i * P:(i + 1) * P],
                              columns(w_fi, tile * P + i * FFN, n=P))
            return self.load(half(0), half(1))

        def hidden(slot, nxt, pending, turn, dst, between=None):
            banks = (2 * turn, 2 * turn + 1)
            done = self.unit(slot, self.plan([self.b(i, S) for i in banks], S), nxt, pending,
                             free=[f"bank{i} read" for i in banks], ready=self.READY, between=between)
            b = turn % 2
            g, full = self.tmp[:, b, 0:S], self.tmp2[:, b, 0:S]
            a = act.do(lambda e: e.activation(g, self.b(banks[0], S), ACT.Silu), done, f"silu{b} read")
            p.note(f"bank{banks[0]} read", a)
            t = dve.do(lambda e: e.tensor_tensor(full, g, self.b(banks[1], S), ALU.mult), a)
            p.note(f"bank{banks[1]} read", t)
            p.note(f"silu{b} read", t)
            high, low = flat(fh[:, bass.ds(dst, 1), :]), flat(fl[:, bass.ds(dst, 1), :])
            t = dve.do(lambda e: e.tensor_copy(high, full), t, "hidden free")
            t = dve.do(lambda e: e.tensor_tensor(low, full, high.bitcast(F32), ALU.subtract), t)
            p.note("hidden made", t)

        for part in range(2):
            def in_body(it):
                slots = [hidden_load(it * 4 + j + 16 * part) for j in range(4)]
                for j in range(4):
                    hidden(slots[j], slots[(j + 1) % 4], j == 3, j % 2, it * 4 + j)
            p.repeat(4, in_body)

            def out_body(it):
                slots = [self.load_columns(w_fo, (it * 4 + j) * 256, 16 * part) for j in range(4)]
                for j in range(4):
                    banks = (2 * (j % 2), 2 * (j % 2) + 1)
                    done = self.unit(slots[j], self.plan([self.b(i, S) for i in banks], S, ah=fh, al=fl),
                                     slots[(j + 1) % 4], j == 3, free=[f"bank{i} read" for i in banks],
                                     ready=["hidden made"])
                    for i in range(2):
                        dst = flat(y[:, bass.ds((it * 4 + j) * 2 + i, 1), 0:S])
                        if part == 0:
                            t = act.do(lambda e: e.activation(dst, self.b(banks[i], S), ACT.Copy), done)
                        else:
                            t = dve.do(lambda e: e.tensor_tensor(dst, dst, self.b(banks[i], S), ALU.add), done)
                        p.note(f"bank{banks[i]} read", t)
                p.note("hidden free", done)
            p.repeat(2, out_body)
            if part == 0:
                dve.wait(Token(act.done, act.done.count, None))

        def last_body(it):
            slots = [hidden_load(it * 3 + j + 32) for j in range(3)] + [self.load_columns(w_ada, (it + 44) * 256)]
            for j in range(3):
                between = (lambda q: self.ada_step(slots[3], 0, q + 8 * j, n=1)) if j < 2 else None
                hidden(slots[j], slots[(j + 1) % 3], j == 2, j, it * 3 + j, between=between)
            self.ada_columns(0, it + 44)
        p.repeat(4, last_body)
        p.note("operand free", Token(self.used, self.used.count, None))
        self.ada_take(88, 96)
        self.pe.wait("bank7 read")

        def block_load(u):
            def half(i):
                h = 2 * u + i
                k0, c0 = 32 + 4 * (h % 3), 512 * (h // 3)
                return (lambda r: r[:, i * 2048:(i + 1) * 2048].rearrange("p (k n) -> p k n", n=512),
                        columns(w_fo, c0, k0, 4, 512))
            return self.load(half(0), half(1))
        slots = [block_load(u) for u in range(4)]
        after = (self.units + 2) % SLOTS
        for u in range(6):
            plan, free = [], []
            for q in range(8):
                e8 = 8 * u + q
                blk, kt = e8 // 12, e8 % 12
                banks = [4 * (blk % 2) + j for j in range(4)]
                if kt == 0:
                    free += [f"bank{j} read" for j in banks]
                plan.append([(self.b(banks[j], S), (lambda j: lambda w: w[:, j * P:(j + 1) * P])(j), fh[:, kt, :],
                              fl[:, kt, :], kt == 0, kt == 11) for j in range(4)])
            done = self.unit(slots[u], plan, slots[u + 1] if u < 5 else after, pending=u == 5, free=free,
                             ready=["hidden made"])
            if u < 2:
                slots.append(block_load(u + 4))
            for blk in range(4):
                if (12 * blk + 11) // 8 == u:
                    for j in range(4):
                        bank, dst = 4 * (blk % 2) + j, y[:, 4 * blk + j, 0:S]
                        t = dve.do(lambda e: e.tensor_tensor(dst, dst, self.b(bank, S), ALU.add), done)
                        p.note(f"bank{bank} read", t)


    def attention1(self):
        p, pe, act, dve, pool, proj = self.p, self.pe, self.act, self.dve, self.pool, self.proj
        a0 = self.big + 47104
        kd = self.sb("kd", [P, 2, 2, S], at=a0)
        vt = proj[:, 8, :].rearrange("p (i d) -> p i d", i=2)
        pt = self.sb("pt1", [P, 4, 384], at=a0 + 4096)
        pm = self.sb("pm1", [P, 2, 4, 384], at=self.work)
        st = self.sb("st1", [P, 2, 6, 8], at=self.work + 12288)
        bcast = lambda ap, n: ap.unsqueeze(1).broadcast_to([P, n, S])
        turned = None
        for n, t0 in enumerate((8, 0, 2, 4, 6)):
            w = 1 if t0 == 8 else 2
            bank = 6 + n % 2
            xs = proj[:, t0:t0 + w, :]
            ps = self.b(bank, w * S).rearrange("p (a b) -> p a b", a=w)
            r = pe.do(lambda e: e.matmul(self.b(bank, w * S), self.C("rot1"), flat(xs), start=True, stop=True),
                      f"bank{bank} read", self.trig)
            tmp = pm[:, n % 2, 0:2, 0:S][:, 0:w, :]
            s = dve.do(lambda e: e.tensor_tensor(tmp, ps, bcast(self.sin1, w), ALU.mult), r, f"rope{n % 2}")
            p.note(f"bank{bank} read", s)
            q = pool.do(lambda e: e.tensor_tensor(xs, xs, bcast(self.cos1, w), ALU.mult), r, self.trig)
            turned = dve.do(lambda e: e.tensor_tensor(xs, xs, tmp, ALU.add), s, q)
            p.note(f"rope{n % 2}", turned)
            if t0 == 8:
                k_done = turned
        kd_zero = pool.do(lambda e: e.memset(kd[:, :, :, :], 0.0))
        for kv in range(2):
            for half in range(2):
                act.do(lambda e: e.activation(kd[64 * half:64 * half + 64, kv, half, :],
                                              proj[64 * kv:64 * kv + 64, 8, :], ACT.Copy), k_done, kd_zero)
        kd_done = Token(act.done, act.done.count, None)

        def v_turn(e):
            for i in range(2):
                last = e.transpose(self.b(4, P, i * P), proj[:, 9, i * P:(i + 1) * P], self.C("ident"))
            return last
        t = pe.do(v_turn)
        v_done = act.do(lambda e: e.activation(flat(vt), self.b(4, 2 * P), ACT.Copy), t, kd_done)
        p.note("bank4 read", v_done)
        pe.wait(turned, kd_done, v_done)
        scale = 64 ** -0.5
        span = lambda u: (3 * u, 3 * u + 3)

        def scores(g):
            u, kv = g % 2, g // 2
            lo = 3 * u

            def products(e):
                for h in range(4):
                    q = lambda blk: proj[:, (4 * g + h) // 2, blk * P:(blk + 1) * P]
                    e.matmul(self.b(lo, P, h * P), q(0), kd[:, kv, h % 2, 0:P], start=True, stop=True)
                    last = e.matmul(self.b(lo + 1 + h // 2, S, (h % 2) * S), q(1), kd[:, kv, h % 2, :],
                                    start=True, stop=True)
                return last
            t = pe.do(products, *[f"bank{i} read" for i in range(lo, lo + 3)])
            own = self.C("own").unsqueeze(1).broadcast_to([P, 4, P])
            both = self.cs[:, self.cat["prev"][0]:self.cat["own"][1]].unsqueeze(1).broadcast_to([P, 4, S])
            near, far = pm[:, u, :, 0:P], pm[:, u, :, P:384]
            a = dve.do(lambda e: e.scalar_tensor_tensor(
                out=near, in0=self.b(lo, 512).rearrange("p (h k) -> p h k", h=4), scalar=scale, in1=own, op0=ALU.mult,
                op1=ALU.add), t, f"pm{u} read")
            b = dve.do(lambda e: e.scalar_tensor_tensor(
                out=far, in0=self.bank[:, lo + 1:lo + 3, :].rearrange("p a (h k) -> p (a h) k", h=2), scalar=scale,
                in1=both, op0=ALU.mult, op1=ALU.add), t)
            for i in range(lo, lo + 3):
                p.note(f"bank{i} read", b)
            mx, neg, sums, es, den = (st[:, u, i, :] for i in range(5))
            dve.do(lambda e: e.tensor_reduce(mx[:, 0:4], near, AX.X, ALU.max), a)
            t = dve.do(lambda e: e.tensor_reduce(mx[:, 4:8], far, AX.X, ALU.max), b)
            sink = self.sinks[:, 4 * g:4 * g + 4].unsqueeze(1).broadcast_to([P, 2, 4])
            two = lambda ap: ap.rearrange("p (b h) -> p b h", b=2)
            t = dve.do(lambda e: e.tensor_tensor(two(mx), two(mx), sink, ALU.max), t)
            t = dve.do(lambda e: e.tensor_scalar(neg, mx, -1.0, None, ALU.mult), t)
            d = dve.do(lambda e: e.tensor_tensor(two(es), two(neg), sink, ALU.add), t)
            for h in range(4):
                act.do(lambda e: e.activation(pm[:, u, h, 0:P], pm[:, u, h, 0:P], ACT.Exp, bias=neg[:, h:h + 1],
                                              accum_out=sums[:, h:h + 1]), d)
                act.do(lambda e: e.activation(pm[:, u, h, P:384], pm[:, u, h, P:384], ACT.Exp,
                                              bias=neg[:, 4 + h:5 + h], accum_out=sums[:, 4 + h:5 + h]))
            t = act.do(lambda e: e.activation(es, es, ACT.Exp))
            t = dve.do(lambda e: e.tensor_tensor(den, sums, es, ALU.add), t)
            t = dve.do(lambda e: e.reciprocal(den, den), t)
            over = lambda lo, n: den[:, lo:lo + 4].unsqueeze(2).broadcast_to([P, 4, n])
            pool.do(lambda e: e.tensor_tensor(near, near, over(0, P), ALU.mult), t)
            return pool.do(lambda e: e.tensor_tensor(far, far, over(4, S), ALU.mult))

        def values(g, weights):
            u, kv = g % 2, g // 2
            lo = 3 * u

            def turn(e):
                for h in range(4):
                    for j in range(3):
                        n = 3 * h + j
                        last = e.transpose(self.b(lo + n // 4, P, (n % 4) * P), pm[:, u, h, j * P:(j + 1) * P],
                                           self.C("ident"))
                return last
            t = pe.do(turn, weights, *[f"bank{i} read" for i in range(lo, lo + 3)])
            p.note(f"pm{u} read", t)
            t = act.do(lambda e: e.activation(flat(pt[:, :, :]), self.bank[:, lo:lo + 3, :].rearrange("p a b -> p (a b)"),
                                              ACT.Copy), t, "pt read")
            for i in range(lo, lo + 3):
                p.note(f"bank{i} read", t)

            def products(e):
                for h in range(4):
                    po = 64 * (h % 2)
                    v = lambda blk: vt[:, blk, kv * 64:kv * 64 + 64]
                    o = lambda blk: self.b(6, P, (h // 2) * S + blk * P, p=64, p0=po)
                    e.matmul(o(0), v(0), pt[:, h, 0:P], start=True, stop=True, skip_group_check=True)
                    e.matmul(o(1), v(0), pt[:, h, P:2 * P], start=True, stop=False, skip_group_check=True)
                    last = e.matmul(o(1), v(1), pt[:, h, 2 * P:3 * P], start=False, stop=True, skip_group_check=True)
                return last
            t = pe.do(products, t, "bank6 read")
            p.note("pt read", t)
            t = act.do(lambda e: e.activation(flat(proj[:, 2 * g:2 * g + 2, :]), self.b(6, 512), ACT.Copy), t)
            p.note("bank6 read", t)

        ready = scores(0)
        for g in range(1, 4):
            nxt = scores(g)
            values(g - 1, ready)
            ready = nxt
        values(3, ready)

    def hgrn(self):
        p, pe, act, dve, pool, proj = self.p, self.pe, self.act, self.dve, self.pool, self.proj
        N = 4 * S
        qk = self.sb("qk", [P, 2, N], at=self.work)
        qx = self.sb("qx", [P, 4, 6, CH], at=self.work + 8192)
        a0 = self.big + 43008
        b = self.sb("b", [P, N], at=a0)
        comp = self.sb("comp", [P, 8, CH], at=a0 + 4096)
        sc = self.sb("sc", [P, 4, 384], at=a0 + 6144)
        lb = self.sb("lb", [P, 3, 8], at=self.work + 14336)
        mask = proj[:, 8, :]
        d = dve.do(lambda e: e.tensor_tensor(lb[:, 2, :], self.vec[:, 0, 80:88], self.vec[:, 0, 88:96], ALU.subtract))
        low = act.do(lambda e: e.activation(lb[:, 0, :], lb[:, 2, :], ACT.Sigmoid), d)
        act.do(lambda e: e.activation(flat(proj[:, 18:26, :]), flat(proj[:, 18:26, :]), ACT.Sigmoid))
        sig = act.do(lambda e: e.activation(flat(proj[:, 34:42, :]), flat(proj[:, 34:42, :]), ACT.Sigmoid))
        q_done = act.do(lambda e: e.activation(flat(proj[:, 10:18, :]), flat(proj[:, 10:18, :]), ACT.Silu))
        om = dve.do(lambda e: e.tensor_scalar(lb[:, 1, :], lb[:, 0, :], -1.0, 1.0, ALU.mult, ALU.add), low)
        t = pool.do(lambda e: e.memset(mask, 1.0))
        mask_done = pool.do(lambda e: e.memset(mask.rearrange("p (c n) -> p c n", n=CH)[:, :, 0:1], 0.0), t)
        for h in range(8):
            f = dve.do(lambda e: e.tensor_scalar(proj[:, 18 + h, :], proj[:, 18 + h, :], lb[:, 1, h:h + 1],
                                                 lb[:, 0, h:h + 1], ALU.mult, ALU.add), om, sig)
        for bk in range(4):
            def turn(e):
                for j in range(4):
                    h, i = 2 * bk + j // 2, j % 2
                    last = e.transpose(self.b(bk, P, j * P), proj[:, 26 + h, i * P:(i + 1) * P], self.C("ident"))
                return last
            t = pe.do(turn, f"bank{bk} read")
            t = act.do(lambda e: e.activation(flat(proj[:, 26 + 2 * bk:28 + 2 * bk, :]), self.b(bk, 512), ACT.Copy), t)
            p.note(f"bank{bk} read", t)
        v_done = t
        for hf in range(2):
            heads = [4 * hf + i for i in range(4)]
            q, key = flat(proj[:, 10 + 4 * hf:14 + 4 * hf, :]), flat(proj[:, 18 + 4 * hf:22 + 4 * hf, :])
            t = act.do(lambda e: e.activation(b[:, :], key, ACT.Ln), f, "b read")
            k_done = dve.do(lambda e: e.tensor_scalar(key, key, -1.0, 1.0, ALU.mult, ALU.add), t)
            for h in range(4):
                bh = b[:, h * S:(h + 1) * S]
                scan = dve.do(lambda e: e.tensor_tensor_scan(bh, mask, bh, 0.0, ALU.mult, ALU.add), t, mask_done)
            zero = pool.do(lambda e: e.memset(comp[:, :, :], 0.0), "comp read")
            pe.wait(k_done, q_done)

            def blocks(left, right, bank):
                def products(e):
                    for h in range(4):
                        for ch in range(NCH):
                            lo = h * S + ch * CH
                            last = e.matmul(self.b(bank, CH, (2 * h + ch // 2) * CH, p=CH, p0=CH * (ch % 2)),
                                            left[:, lo:lo + CH], right[:, lo:lo + CH], start=True, stop=True,
                                            skip_group_check=True)
                    return last
                return products
            for li, m in enumerate((0, 32, 16, 8, 4, 2, 1)):
                bank = 2 * hf + li % 2
                if m == 0:
                    t = pe.do(blocks(key, q, bank), f"bank{bank} read")
                    name = "diag"
                else:
                    u, name = li % 2, f"lvl{m}"
                    buf = qk[:, u, :]
                    view = lambda ap: ap.rearrange("p (n t) -> p n t", t=2 * m)
                    mid = view(b[:, :])[:, :, m - 1:m].broadcast_to([P, N // (2 * m), 2 * m])
                    t = pool.do(lambda e: e.tensor_tensor(view(buf), view(b[:, :]), mid, ALU.subtract), scan,
                                f"qk{u} read")
                    left, right = view(buf)[:, :, 0:m], view(buf)[:, :, m:2 * m]
                    act.do(lambda e: e.activation(left, left, ACT.Exp, scale=-1.0), t)
                    t = act.do(lambda e: e.activation(right, right, ACT.Exp))
                    dve.do(lambda e: e.tensor_tensor(left, left, view(key)[:, :, 0:m], ALU.mult), t)
                    t = dve.do(lambda e: e.tensor_tensor(right, right, view(q)[:, :, m:2 * m], ALU.mult), q_done)
                    t = pe.do(blocks(buf, buf, bank), t, f"bank{bank} read")
                    p.note(f"qk{u} read", t)
                lvl = self.C(name).bitcast(U32).unsqueeze(1).broadcast_to([P, 8, CH])
                t = dve.do(lambda e: e.copy_predicated(comp[:, :, :], lvl,
                                                       self.b(bank, 512).rearrange("p (a t) -> p a t", t=CH)), t, zero)
                p.note(f"bank{bank} read", t)
            comp_done = t
            eb, kend = qk[:, 0, :], qk[:, 1, :]
            chunks = lambda ap: ap.rearrange("p (n t) -> p n t", t=CH)
            t = pool.do(lambda e: e.tensor_tensor(chunks(kend), chunks(b[:, :])[:, :, CH - 1:CH].broadcast_to([P, 16, CH]),
                                                  chunks(b[:, :]), ALU.subtract), "qk1 read")
            e1 = act.do(lambda e: e.activation(eb, b[:, :], ACT.Exp), "qk0 read")
            t = act.do(lambda e: e.activation(kend, kend, ACT.Exp), t)
            p.note("b read", t)
            kend_done = dve.do(lambda e: e.tensor_tensor(kend, kend, key, ALU.mult), t)
            by = lambda ap: ap.rearrange("p (h c t) -> p h c t", h=4, t=CH)
            dec = lambda ch: by(eb)[:, :, ch, CH - 1:CH].broadcast_to([P, 4, CH])
            for seg, ch in ((0, 3), (1, 2), (3, 1)):
                t = pool.do(lambda e: e.tensor_tensor(qx[:, :, seg, :], by(q)[:, :, ch, :], by(eb)[:, :, ch, :], ALU.mult),
                            e1, "qx read")
            for seg, src, ch in ((2, 0, 2), (4, 1, 1), (5, 2, 1)):
                t = pool.do(lambda e: e.tensor_tensor(qx[:, :, seg, :], qx[:, :, src, :], dec(ch), ALU.mult), t)

            def between(e):
                for h in range(4):
                    out = lambda n, lo, p0: self.b(4 + h // 2, n, (h % 2) * S + lo, p=CH, p0=p0)
                    src = lambda ch: kend[:, h * S + ch * CH:h * S + (ch + 1) * CH]
                    tgt = lambda lo, hi: qx[:, h, lo:hi, :].rearrange("p a b -> p (a b)")
                    e.matmul(out(3 * CH, 0, 0), src(0), tgt(3, 6), start=True, stop=True, skip_group_check=True)
                    e.matmul(out(2 * CH, 0, CH), src(1), tgt(1, 3), start=True, stop=True, skip_group_check=True)
                    last = e.matmul(out(CH, 3 * CH, 0), src(2), tgt(0, 1), start=True, stop=True, skip_group_check=True)
                return last
            t = pe.do(between, kend_done, t, "bank4 read", "bank5 read")
            for name in ("qk0 read", "qk1 read", "qx read"):
                p.note(name, t)
            ps = self.bank[:, 4:6, :].rearrange("p a (h n) -> p (a h) n", n=S)
            cp = comp[:, :, :].rearrange("p (h i) n -> p h i n", i=2)
            lo, hi = slice(0, CH), slice(CH, P)
            dve.do(lambda e: e.memset(sc[hi, :, 0:CH], 0.0), "sc read")
            z = dve.do(lambda e: e.memset(sc[hi, :, 256:320], 0.0))
            act.do(lambda e: e.activation(sc[lo, :, 64:256], ps[lo, :, 0:192], ACT.Copy), t, "sc read")
            act.do(lambda e: e.activation(sc[lo, :, 320:384], ps[lo, :, 192:256], ACT.Copy))
            a = act.do(lambda e: e.activation(sc[hi, :, 128:256], ps[hi, :, 0:128], ACT.Copy))
            p.note("bank4 read", a)
            p.note("bank5 read", a)
            for i in range(2):
                dve.do(lambda e: e.tensor_copy(sc[lo, :, 256 * i:256 * i + 64], cp[lo, :, i, :]), comp_done, "sc read")
                c = dve.do(lambda e: e.tensor_copy(sc[hi, :, 256 * i + 64:256 * i + 128], cp[hi, :, i, :]))
            p.note("comp read", c)

            def outs(e):
                for h in range(4):
                    o = lambda lo, n: self.b(6 + h // 2, n, (h % 2) * S + lo)
                    v = lambda i: proj[:, 26 + 4 * hf + h, i * P:(i + 1) * P]
                    e.matmul(o(0, S), v(0), sc[:, h, 0:S], start=True, stop=False, skip_group_check=True)
                    last = e.matmul(o(P, P), v(1), sc[:, h, S:384], start=False, stop=True, skip_group_check=True)
                return last
            t = pe.do(outs, z, a, c, v_done, "bank6 read", "bank7 read")
            p.note("sc read", t)
            t = act.do(lambda e: e.activation(q, self.bank[:, 6:8, :].rearrange("p a b -> p (a b)"), ACT.Copy), t)
            p.note("bank6 read", t)
            p.note("bank7 read", t)
        for hf in range(2):
            o = flat(proj[:, 10 + 4 * hf:14 + 4 * hf, :])
            sq = qk[:, 0, :]
            t = act.do(lambda e: e.activation(sq, o, ACT.Square), t, "qk0 read")

            def sums(e):
                for j in range(2):
                    last = e.matmul(self.b(j, 512), self.C("ones"), sq[:, j * 512:(j + 1) * 512], start=True, stop=True)
                return last
            m = pe.do(sums, t, "bank0 read", "bank1 read")
            p.note("qk0 read", m)
            rs = qk[:, 1, :]
            t = act.do(lambda e: e.activation(rs, self.bank[:, 0:2, :].rearrange("p a b -> p (a b)"), ACT.Sqrt,
                                              bias=self.col[:, 0:1], scale=1.0 / P), m, "rs used")
            p.note("bank0 read", t)
            p.note("bank1 read", t)
            d = dve.do(lambda e: e.reciprocal(rs, rs), t)
            d = dve.do(lambda e: e.tensor_tensor(o, o, rs, ALU.mult), d)
            p.note("rs used", d)
            d = dve.do(lambda e: e.scalar_tensor_tensor(out=o, in0=o, scalar=self.vec[:, 1, 54:55],
                                                        in1=flat(proj[:, 34 + 4 * hf:38 + 4 * hf, :]), op0=ALU.mult,
                                                        op1=ALU.mult), d)

    def second_block(self, w_in, w_out, w_gla, w_gla_out):
        p, pe, act, dve, y = self.p, self.pe, self.act, self.dve, self.y
        proj = self.proj = self.sb("proj2", [P, 48, T2], at=self.big)
        y2 = self.y = self.sb("y2", [P, KT, T2], at=self.big)

        def project(w):
            def body(it):
                slots = [self.load_columns(w, (it * 4 + j) * 256) for j in range(4)]
                for j in range(4):
                    banks = (2 * (j % 2), 2 * (j % 2) + 1)
                    done = self.unit(slots[j], self.plan([self.b(i) for i in banks], T2), slots[(j + 1) % 4], j == 3,
                                     free=[f"bank{i} read" for i in banks], ready=self.READY)
                    for i in range(2):
                        t = act.do(lambda e: e.activation(flat(proj[:, bass.ds((it * 4 + j) * 2 + i, 1), :]),
                                                          self.b(banks[i]), ACT.Copy), done)
                        p.note(f"bank{banks[i]} read", t)
                p.note("operand free", done)
            p.repeat(6, body)

        project(w_in)
        self.join()
        self.rope2(0, 8, self.vec[:, 1, 52:53])
        self.rope2(16, 4, self.vec[:, 1, 53:54])
        self.join()
        self.attention2()
        self.join()
        g = flat(proj[:, 32:48, :])
        sg = act.do(lambda e: e.activation(g, g, ACT.Silu))
        for kt in range(KT):
            full = self.tmp[:, kt % 2, :]
            t = dve.do(lambda e: e.tensor_tensor(full, proj[:, kt, :], proj[:, 32 + kt, :], ALU.mult), sg)
            h = act.do(lambda e: e.activation(self.ah[:, kt, :], full, ACT.Copy), t)
            t = dve.do(lambda e: e.tensor_tensor(self.al[:, kt, :], full, self.ah[:, kt, :].bitcast(F32),
                                                 ALU.subtract), h)
            if kt % 2:
                p.note(f"operand {kt // 2}", t)
        self.join()
        summed = self.to_y(w_out, T2)
        self.join()
        rs = self.residual(T2, T2, y2, None, self.vec[:, 1, 0:16], summed)
        self.operand(T2, self.rs2, self.vec[:, 0, 112:128], None, rs)
        self.join()

        pe.wait(Token(self.low_in, self.low_in.count, None))

        def low_rank(e):
            for kt in range(KT):
                for a in (self.ah, self.al):
                    last = e.matmul(self.b(5, p=32), self.wlr[:, kt, :], a[:, kt, :].bitcast(F32),
                                    start=kt == 0 and a is self.ah, stop=kt == KT - 1 and a is self.al,
                                    skip_group_check=True)
            return last
        lr = self.lr = self.sb("lr", [32, T2], at=self.work)
        t = pe.do(low_rank)
        self.lr_done = act.do(lambda e: e.activation(lr[:, :], self.b(5, p=32), ACT.Copy), t)
        project(w_gla)
        self.join()
        self.gla()
        self.join()
        summed = self.to_y(w_gla_out, T2, last=True)
        self.join()
        r = self.rstd(6, S, D, self.rs[:, 0:S], summed)
        for kt in range(KT):
            t = kt % 2
            tmp = self.tmp[:, t, 0:S]
            a = self.pool.do(lambda e: e.tensor_tensor(tmp, y2[:, kt, 0:S], self.rs[:, 0:S], ALU.mult), r,
                             f"tmp{t} read")
            f = dve.do(lambda e: e.scalar_tensor_tensor(out=self.X[:, kt, 0:S], in0=tmp,
                                                        scalar=self.vec[:, 1, 16 + kt:17 + kt],
                                                        in1=self.X[:, kt, 0:S], op0=ALU.mult, op1=ALU.add), a)
            p.note(f"tmp{t} read", f)
        self.x_done = f

    def rope2(self, first, n, gain):
        p, pe, act, dve, pool, proj = self.p, self.pe, self.act, self.dve, self.pool, self.proj
        xg = self.sb(f"xg{first}", [P, 2, T2], at=self.ah_at)
        rt = self.sb(f"rt{first}", [P, 2, T2], at=self.ah_at + 2176)
        rs = self.sb(f"rsh{first}", [P, 2, T2], at=self.ah_at + 4352)

        def body(it):
            for u in range(2):
                x = flat(proj[:, bass.ds(it * 2 + first + u, 1), :])
                g, r, s = xg[:, u, :], rt[:, u, :], rs[:, u, :]
                a = act.do(lambda e: e.activation(self.sq[:, u, :], x, ACT.Square), f"hsq{u} read")
                m = pe.do(lambda e: e.matmul(self.b(4 + u), self.C("ones"), self.sq[:, u, :], start=True, stop=True),
                          a, f"bank{4 + u} read")
                p.note(f"hsq{u} read", m)
                b = act.do(lambda e: e.activation(g, x, ACT.Copy, scale=gain), f"xg{u} read")
                w = pe.do(lambda e: e.matmul(self.b(6 + u), self.C("rot2"), g, start=True, stop=True), b,
                          f"bank{6 + u} read")
                t = act.do(lambda e: e.activation(s, self.b(4 + u), ACT.Sqrt, bias=self.col[:, 0:1], scale=1.0 / P), m,
                           f"rsh{u} read")
                p.note(f"bank{4 + u} read", t)
                t = dve.do(lambda e: e.reciprocal(s, s), t)
                d = dve.do(lambda e: e.tensor_tensor(r, self.b(6 + u), self.C("sin2"), ALU.mult), w)
                p.note(f"bank{6 + u} read", d)
                c = pool.do(lambda e: e.tensor_tensor(g, g, self.C("cos2"), ALU.mult), w)
                d = dve.do(lambda e: e.tensor_tensor(r, r, g, ALU.add), c, d)
                p.note(f"xg{u} read", d)
                d = dve.do(lambda e: e.tensor_tensor(x, r, s, ALU.mult), d, t)
                p.note(f"rsh{u} read", d)
        p.repeat(n, body)

    def attention2(self):
        p, pe, act, dve, pool, proj = self.p, self.pe, self.act, self.dve, self.pool, self.proj
        at = self.ah_at

        def sb(name, shape):
            nonlocal at
            r = self.sb(name, shape, at=at)
            at += 4 * int(np.prod(shape[1:]))
            assert at <= self.ah_at + 2 * 4 * KT * T2
            return r
        qs, ks, vs = sb("qs", [P, 2, 2, T2]), sb("ks", [P, 2, T2]), sb("vs", [P, T2])
        vt, pm, pl = sb("vt2", [P, 2, 3, P]), sb("pm2", [P, 2, 4, T2]), sb("pl2", [32, 2, T2])
        pt, st, qm = sb("pt2", [P, 3, 544]), sb("st2", [P, 2, 4, 8]), sb("qm", [P, 2, 2, META])
        scale = P ** -0.5
        toks = (P, P, META)

        def weights(i, u):
            q = pool.do(lambda e: e.tensor_copy(flat(qs[:, u, :, :]), flat(proj[:, bass.ds(i * 2, 2), :])), f"qs{u} read")
            pool.do(lambda e: e.tensor_copy(qm[:, u, :, :], proj[:, bass.ds(i * 2, 2), S:T2]), f"qs{u} read")
            pool.do(lambda e: e.tensor_copy(ks[:, u, :], flat(proj[:, bass.ds(i + 16, 1), :])))
            v = pool.do(lambda e: e.tensor_copy(vs[:, :], flat(proj[:, bass.ds(i + 24, 1), :])), "vs read")

            def v_turn(e):
                for j, n in enumerate(toks):
                    last = e.transpose(self.b(3, P, j * P, p=n), vs[:, j * P:j * P + n], self.C("ident"))
                return last
            t = pe.do(v_turn, v, "bank3 read")
            p.note("vs read", t)
            act.do(lambda e: e.activation(flat(vt[:, u, 0:2, :]), self.b(3, 2 * P), ACT.Copy), t, f"vt{u} read")
            t = act.do(lambda e: e.activation(vt[0:META, u, 2, :], self.b(3, P, 2 * P, p=META), ACT.Copy))
            p.note("bank3 read", t)
            p.note(f"vt{u} made", t)
            for n in range(5):
                bank = n % 3
                rows = P if n < 4 else 32
                lhs = qs[:, u, n // 2, (n % 2) * P:(n % 2) * P + P] if n < 4 else flat(qm[:, u, :, :])
                t = pe.do(lambda e: e.matmul(self.b(bank, p=rows), lhs, ks[:, u, :], start=True, stop=True), v,
                          f"bank{bank} read")
                mx, neg, sm, rec = (st[0:rows, u, j, n:n + 1] for j in range(4))
                t = dve.do(lambda e: e.tensor_reduce(mx, self.b(bank, p=rows), AX.X, ALU.max), t)
                t = dve.do(lambda e: e.tensor_scalar(neg, mx, -scale, None, ALU.mult), t)
                dst = pm[:, u, n, :] if n < 4 else pl[:, u, :]
                t = act.do(lambda e: e.activation(dst, self.b(bank, p=rows), ACT.Exp, bias=neg, scale=scale,
                                                  accum_out=sm), t, f"pm{u} turned")
                p.note(f"bank{bank} read", t)
                r = dve.do(lambda e: e.reciprocal(rec, sm), t)
                last = pool.do(lambda e: e.tensor_tensor(dst, dst, rec.broadcast_to([rows, T2]), ALU.mult), r)
            p.note(f"qs{u} read", Token(pe.done, pe.done.count, p.loop))
            p.note(f"weights{u} made", last)

        def values(i, u):
            def turn(j, bank):
                def products(e):
                    for n in range(4):
                        last = e.transpose(self.b(bank, P, n * P, p=toks[j]), pm[:, u, n, j * P:j * P + toks[j]],
                                           self.C("ident"))
                    return last
                return products

            def turn_meta(e):
                for j in range(3):
                    last = e.transpose(self.b(3, 32, j * 32, p=toks[j]), pl[:, u, j * P:j * P + toks[j]],
                                       self.cs[0:32, self.cat["ident"][0]:self.cat["ident"][0] + 32])
                return last
            pe.wait(f"weights{u} made")
            t = pe.do(turn_meta, "bank3 read")
            act.do(lambda e: e.activation(pt[:, 0:2, 512:544], self.b(3, 64).rearrange("p (a b) -> p a b", a=2),
                                          ACT.Copy), t, "pt read")
            t = act.do(lambda e: e.activation(pt[0:META, 2, 512:544], self.b(3, 32, 64, p=META), ACT.Copy))
            p.note("bank3 read", t)
            for j in range(3):
                bank, rows = 4 + j % 2, toks[j]
                t = pe.do(turn(j, bank), f"bank{bank} read")
                if j == 2:
                    p.note(f"pm{u} turned", t)
                if j == 1:
                    dve_t = dve.do(lambda e: e.tensor_copy(pt[:, 1, 0:512], self.b(bank, 512)), t, "pt read")
                    p.note(f"bank{bank} read", dve_t)
                else:
                    t = act.do(lambda e: e.activation(pt[0:rows, j, 0:512], self.b(bank, 512, p=rows), ACT.Copy), t)
                    p.note(f"bank{bank} read", t)

            def outs(e):
                for bank, lo, hi in ((6, 0, 512), (7, 512, 544)):
                    for j in range(3):
                        last = e.matmul(self.b(bank, hi - lo), vt[0:toks[j], u, j, :], pt[0:toks[j], j, lo:hi],
                                        start=j == 0, stop=j == 2, skip_group_check=True)
                return last
            t = pe.do(outs, t, dve_t, f"vt{u} made", "bank6 read", "bank7 read")
            p.note("pt read", t)
            p.note(f"vt{u} read", t)
            act.do(lambda e: e.activation(proj[:, bass.ds(i * 2, 2), 0:S],
                                          self.b(6, 512).rearrange("p (a b) -> p a b", a=2), ACT.Copy), t)
            t = act.do(lambda e: e.activation(proj[:, bass.ds(i * 2, 2), S:T2],
                                              self.b(7, 32).rearrange("p (a b) -> p a b", a=2), ACT.Copy))
            p.note("bank6 read", t)
            p.note("bank7 read", t)

        weights(0, 0)

        def body(it):
            weights(it * 2 + 1, 1)
            values(it * 2, 0)
            weights(it * 2 + 2, 0)
            values(it * 2 + 1, 1)
        p.repeat(3, body)
        weights(7, 1)
        values(6, 0)
        values(7, 1)

    def gla(self):
        p, pe, act, dve, pool, proj = self.p, self.pe, self.act, self.dve, self.pool, self.proj
        A = self.ah_at
        gf = self.sb("gf", [P, 8, T2], at=A)
        gb = self.sb("gb", [P, 8, T2], at=A + 8704)
        tt = self.sb("tt", [P, 8, T2], at=A + 17408)
        ex = self.sb("ex", [P, 4, 2, T2], at=A + 17408)
        vv = self.sb("vv", [P, 3, 512], at=A + 26112)
        mask = self.sb("mask", [P, T2], at=A + 32256)
        B = self.big + 52224
        F = self.sb("F", [P, 2, 656], at=B)
        G = self.sb("G", [P, 2, 512], at=B + 5248)
        sc = self.sb("sc2", [P, 3, T2], at=B + 9344)
        vs = self.sb("vs2", [P, 4, T2], at=B + 12608)
        kend = self.sb("kend", [P, 2, 2, T2], at=self.tmp_at)
        t = pool.do(lambda e: e.memset(mask[:, :], 1.0))
        mask_done = pool.do(lambda e: e.memset(mask[:, :].rearrange("p (c n) -> p c n", n=16)[:, 0:17:4, 0:1], 0.0), t)
        for d, gg in enumerate((gf, gb)):
            for j in range(8):
                bank = j % 4
                t = pe.do(lambda e: e.matmul(self.b(bank), self.up[:, d, j * P:(j + 1) * P], self.lr[:, :], start=True,
                                             stop=True), f"bank{bank} read", self.lr_done)
                t = dve.do(lambda e: e.tensor_scalar(gg[:, j, :], self.b(bank), self.vec[:, 1, 32 + 8 * d + j:33 + 8 * d + j],
                                                     None, ALU.add), t)
                p.note(f"bank{bank} read", t)
            act.do(lambda e: e.activation(flat(tt[:, :, :]), flat(gg[:, :, :]), ACT.Abs), t, "tt read")
            act.wait(Token(act.done, act.done.count, None))
            t = act.do(lambda e: e.activation(flat(tt[:, :, :]), flat(tt[:, :, :]), ACT.Exp, scale=-1.0))
            t = act.do(lambda e: e.activation(flat(tt[:, :, :]), flat(tt[:, :, :]), ACT.Ln, bias=self.col[:, 1:2]), t)
            t = dve.do(lambda e: e.scalar_tensor_tensor(out=flat(gg[:, :, :]), in0=flat(gg[:, :, :]), scalar=0.0,
                                                        in1=flat(tt[:, :, :]), op0=ALU.min, op1=ALU.subtract), t)
            for j in range(8):
                dst = gf if d == 0 else tt
                s = dve.do(lambda e: e.tensor_tensor_scan(dst[:, j, :], mask[:, :], gg[:, j, :], 0.0, ALU.mult, ALU.add),
                           t, mask_done)
            p.note("tt read", s)
            if d == 1:
                s = pool.do(lambda e: e.tensor_tensor(flat(gb[:, :, :]), flat(gb[:, :, :]), flat(tt[:, :, :]),
                                                      ALU.subtract), s)
                for j in range(8):
                    x4 = lambda ap: ap[:, j, 0:S].rearrange("p (c n) -> p c n", n=CH)
                    dve.do(lambda e: e.tensor_tensor(x4(gb), x4(gb), x4(tt)[:, :, CH - 1:CH].broadcast_to([P, NCH, CH]),
                                                     ALU.add), s)
                s = dve.do(lambda e: e.tensor_tensor(gb[:, :, S:T2], gb[:, :, S:T2],
                                                     tt[:, :, T2 - 1:T2].broadcast_to([P, 8, META]), ALU.add))
        self.join()
        chunk = [(c * CH, CH) for c in range(NCH)] + [(S, META)]
        f_at = {3: 0, 2: 64, 1: 192, 0: 384, 4: 640}
        g_at = {4: 0, 0: 32, 1: 176, 2: 384, 3: 448}
        r = 1.0 / 16

        def body(h):
            two = lambda ap, t0: ap[:, bass.ds(h * 2 + t0, 2), :]
            q, k = two(proj, 0), two(proj, 8)
            e1 = act.do(lambda e: e.activation(ex[:, 0, :, :], two(gf, 0), ACT.Exp, scale=r), "ex read")
            e3 = act.do(lambda e: e.activation(ex[:, 1, :, :], two(gf, 0), ACT.Exp, scale=-r), "heads' keys read")
            e2 = act.do(lambda e: e.activation(ex[:, 2, :, :], two(gb, 0), ACT.Exp, scale=r))
            e4 = act.do(lambda e: e.activation(ex[:, 3, :, :], two(gb, 0), ACT.Exp, scale=-r))
            v = pool.do(lambda e: e.tensor_copy(flat(vs[:, :, :]), flat(proj[:, bass.ds(h * 4 + 16, 4), :])), "vs read")
            for j, n in enumerate((P, P, META)):
                def turn(e):
                    for i in range(4):
                        last = e.transpose(self.b(4 + j, P, i * P, p=n), vs[:, i, j * P:j * P + n], self.C("ident"))
                    return last
                t = pe.do(turn, v, f"bank{4 + j} read")
                a = act.do(lambda e: e.activation(vv[0:n, j, :], self.b(4 + j, 512, p=n), ACT.Copy), t, "vv read")
                p.note(f"bank{4 + j} read", a)
            p.note("vs read", t)
            vv_done = a
            df = lambda c: ex[:, 0, :, chunk[c][0] + chunk[c][1] - 1:chunk[c][0] + chunk[c][1]]
            db = lambda c: ex[:, 2, :, chunk[c][0]:chunk[c][0] + 1]
            dve.wait(e4)
            kf, kb = ex[:, 1, :, :], ex[:, 3, :, :]
            pool.wait(e4)
            a = dve.do(lambda e: e.tensor_tensor(kf, kf, k, ALU.mult))
            b = pool.do(lambda e: e.tensor_tensor(kb, kb, k, ALU.mult))
            dve.wait(a, b, "heads' keys read")
            for d, kk, dec in ((0, kf, df), (1, kb, db)):
                for c in range(5):
                    lo, n = chunk[c]
                    if (d, c) in ((0, 3), (1, 4)):
                        continue
                    t = dve.do(lambda e: e.tensor_tensor(kend[:, d, :, lo:lo + n], kk[:, :, lo:lo + n],
                                                         dec(c).broadcast_to([P, 2, n]), ALU.mult))
            k_done = t
            dve.wait("queries read")
            for c in range(5):
                lo, n = chunk[c]
                for arr, off, d in ((F, f_at[c], 0), (G, g_at[c], 2)):
                    for j in range(2):
                        t = dve.do(lambda e: e.scalar_tensor_tensor(
                            out=arr[:, j, off:off + n], in0=flat(proj[:, bass.ds(h * 2 + j, 1), lo:lo + n]), scalar=r,
                            in1=ex[:, d, j, lo:lo + n], op0=ALU.mult, op1=ALU.mult))
            for src, dst, n, c in ((0, 128, 64, 2), (64, 256, 128, 1), (192, 448, 192, 0)):
                t = pool.do(lambda e: e.tensor_tensor(F[:, :, dst:dst + n], F[:, :, src:src + n],
                                                      df(c).broadcast_to([P, 2, n]), ALU.mult), t)
            t2 = None
            for src, dst, n, c in ((0, 16, 16, 0), (16, 96, 80, 1), (96, 240, 144, 2)):
                t2 = pool.do(lambda e: e.tensor_tensor(G[:, :, dst:dst + n], G[:, :, src:src + n],
                                                       db(c).broadcast_to([P, 2, n]), ALU.mult), t2, t)
            p.note("ex read", t2)

            def scores(e):
                def two_tiles(out, key, query):
                    e.matmul(out, key(0), query(0), start=True, stop=False, skip_group_check=True)
                    return e.matmul(out, key(1), query(1), start=False, stop=True, skip_group_check=True)
                for c in range(5):
                    lo, n = chunk[c]
                    p0, bank = (CH * (c % 2), c // 2)
                    o = lambda to, m, bk=bank: self.b(bk, m, to, p=n, p0=p0)
                    key = lambda a, d: (lambda j: a[:, d, j, lo:lo + n])
                    fq = lambda off, m: (lambda j: F[:, j, off:off + m])
                    gq = lambda off, m: (lambda j: G[:, j, off:off + m])
                    two_tiles(o(lo, n), key(ex, 1), fq(f_at[c], n))
                    last = two_tiles(o((c // 2) * CH, n, 3), key(ex, 3), gq(g_at[c], n))
                    if c == 4:
                        last = two_tiles(o(0, S), key(kend, 0), fq(384, 256))
                        continue
                    if c < 3:
                        last = two_tiles(o(lo + CH, S - lo - CH), key(kend, 0), fq((192, 64, 0)[c], S - lo - CH))
                    g0 = (0, 16, 96, 240)[c]
                    last = two_tiles(o(S, META), key(kend, 1), gq(g0, META))
                    if c:
                        last = two_tiles(o(0, lo), key(kend, 1), gq(g0 + META, lo))
                return last
            t = pe.do(scores, t2, k_done, *[f"bank{i} read" for i in range(4)])
            p.note("heads' keys read", t)
            p.note("queries read", t)
            act.do(lambda e: e.activation(sc[:, 0:2, :], self.bank[:, 0:2, 0:T2], ACT.Copy), t, "sc read")
            a = act.do(lambda e: e.activation(sc[0:META, 2, :], self.b(2, p=META), ACT.Copy))
            dve.settle = True
            for c in range(5):
                lo, n = chunk[c]
                rows = slice(CH * (c % 2), CH * (c % 2) + n)
                lo2, hi2 = self.cat["later"]
                t = dve.do(lambda e: e.copy_predicated(sc[rows, c // 2, lo:lo + n],
                                                       self.cs[rows, lo2:lo2 + n].bitcast(U32),
                                                       self.b(3, n, (c // 2) * CH, p=n, p0=CH * (c % 2))), a)
            dve.settle = False
            for i in range(4):
                p.note(f"bank{i} read", t)

            def outs(e):
                for i in range(4):
                    for j, n in enumerate((P, P, META)):
                        last = e.matmul(self.b(4 + i), vv[0:n, j, i * P:(i + 1) * P], sc[0:n, j, :], start=j == 0,
                                        stop=j == 2)
                return last
            t = pe.do(outs, t, vv_done, *[f"bank{4 + i} read" for i in range(4)])
            p.note("sc read", t)
            p.note("vv read", t)
            for i in range(4):
                act.do(lambda e: e.activation(flat(proj[:, bass.ds(h * 4 + 16 + i, 1), :]), self.b(4 + i), ACT.Copy), t)
                a = act.do(lambda e: e.activation(self.sq[:, i, :], self.b(4 + i), ACT.Square), f"osq{i} read")
                p.note(f"bank{4 + i} read", a)
                m = pe.do(lambda e: e.matmul(self.b(0), self.C("ones"), self.sq[:, i, :], start=i == 0, stop=i == 3), a,
                          *(["bank0 read"] if i == 0 else []))
                p.note(f"osq{i} read", m)
            a = act.do(lambda e: e.activation(flat(proj[:, bass.ds(h * 2, 1), :]), self.b(0), ACT.Copy), m)
            p.note("bank0 read", t, a)
        p.repeat(4, body)
        self.join()
        sums = proj[:, 0:8:2, :]
        t = act.do(lambda e: e.activation(sums, sums, ACT.Sqrt, bias=self.col[:, 0:1], scale=1.0 / 512))
        r_done = dve.do(lambda e: e.reciprocal(sums, sums), t)
        g = flat(proj[:, 32:48, :])
        sg = act.do(lambda e: e.activation(g, g, ACT.Silu))
        for kt in range(KT):
            b = kt % 2
            x, full = self.tmp[:, b, :], self.tmp2[:, b, :]
            t = pool.do(lambda e: e.tensor_tensor(x, proj[:, 16 + kt, :], proj[:, 2 * (kt // 4), :], ALU.mult), r_done,
                        f"tmp{b} read")
            t = dve.do(lambda e: e.scalar_tensor_tensor(out=full, in0=x, scalar=self.vec[:, 1, 48 + kt % 4:49 + kt % 4],
                                                        in1=proj[:, 32 + kt, :], op0=ALU.mult, op1=ALU.mult), t, sg)
            p.note(f"tmp{b} read", t)
            hh = act.do(lambda e: e.activation(self.ah[:, kt, :], full, ACT.Copy), t)
            t = dve.do(lambda e: e.tensor_tensor(self.al[:, kt, :], full, self.ah[:, kt, :].bitcast(F32),
                                                 ALU.subtract), hh)
            if kt % 2:
                p.note(f"operand {kt // 2}", t)

    def finish(self, out):
        p, pe, act, dve, sp = self.p, self.pe, self.act, self.dve, self.sp
        self.join()
        rows = self.sb("out_rows", [P, 2, D], at=self.big + 20000 // 32 * 32)
        stored = p.counter("out_stored")
        view = out[0].rearrange("(i p) d -> p i d", p=P)
        for i in range(2):
            for g in range(4):
                bank = 4 * i + g

                def turn(e):
                    for j in range(4):
                        last = e.transpose(self.b(bank, P, j * P), self.X[:, 4 * g + j, i * P:(i + 1) * P], self.C("ident"))
                    return last
                t = pe.do(turn, f"bank{bank} read")
                eng = (act, dve)[g % 2]
                if g % 2:
                    t = dve.do(lambda e: e.tensor_copy(rows[:, i, g * 512:(g + 1) * 512], self.b(bank, 512)), t)
                else:
                    t = act.do(lambda e: e.activation(rows[:, i, g * 512:(g + 1) * 512], self.b(bank, 512), ACT.Copy), t)
                sp.do(lambda e: e.dma_start(view[:, i, g * 512:(g + 1) * 512], rows[:, i, g * 512:(g + 1) * 512]), t,
                      counter=stored, add=16)
        sp.wait(Token(stored, stored.count, None))


_INS = ['x', 'c', 'positions', 'w_ada', 'b_ada', 'g_pre_mix', 'g_post_mix', 'g_pre_ffn', 'g_post_ffn', 'w_in',
        'attn_sinks', 'w_attn_proj', 'hg_lower_bounds', 'hg_norm', 'w_hgrn_proj', 'w_out', 'w_ffn_in', 'w_ffn_out',
        'meta_tokens_2', 'pre_norm_2', 'post_norm_2', 'attn_w_in_2', 'attn_q_norm_2', 'attn_k_norm_2',
        'attn_w_out_2', 'gla_w_in_2', 'gla_gk_up_2', 'gla_gk_bias_2', 'gla_o_norm_2', 'gla_w_out_2']


def kernel(**inputs):
    import concourse.bacc as _bacc
    from concourse.bass_utils import run_bass_kernel_spmd as _run

    nc = _bacc.Bacc("TRN2", target_bir_lowering=False, num_devices=1, dynamic_dma_scratch_size=1024)
    arrays, args = {}, []
    for name in _INS:
        arrays[f"in_{name}_dram"] = np.ascontiguousarray(inputs[name])
    arrays["consts_dram"] = const_tables()[1]
    for name, a in arrays.items():
        args.append(nc.dram_tensor(name, a.shape, mybir.dt.from_np(a.dtype), kind="ExternalInput").ap())
    args.append(nc.dram_tensor("out_0_dram", (1, S, D), F32, kind="ExternalOutput").ap())
    build(nc, *args)
    r = _run(nc, [arrays], core_ids=[0])
    return r.results[0]["out_0_dram"]
```

```python
import numpy as np
from contextlib import ExitStack

import concourse.bass as bass
from concourse import mybir

F32, F32R, I32, U32 = mybir.dt.float32, mybir.dt.float32r, mybir.dt.int32, mybir.dt.uint32
ACT, ALU, AX = mybir.ActivationFunctionType, mybir.AluOpType, mybir.AxisListType

P = 128
D = 2048
KT = D // P
S = 256
META = 16
T2 = S + META
EPS = 1e-6
SLOTS = 4
UNIT = KT * 256
SUB = UNIT // 8
FFN = 5632
CH = 64
NCH = S // CH
HG = 8


class Counter:

    def __init__(self, sem):
        self.sem, self.count = sem, 0


class Token:

    def __init__(self, counter, value, loop):
        self.counter, self.value, self.loop = counter, value, loop


class Loop:
    def __init__(self, n, steps, before, after):
        self.n, self.steps, self.before, self.after = n, steps, before, after


class Program:

    def __init__(self, nc, ctx):
        self.nc, self.ctx, self.counters = nc, ctx, []
        self.writing, self.loop, self.it, self.events = True, None, 0, {}
        self.always = self.counter("consts_in")
        self.pe, self.act, self.dve, self.pool, self.sp = (
            Engine(self, e, n) for e, n in ((nc.tensor, "pe_done"), (nc.scalar, "act_done"),
                                            (nc.vector, "dve_done"), (nc.gpsimd, "pool_done"), (nc.sync, "sp_done")))

    def counter(self, name):
        self.counters.append(Counter(self.ctx.enter_context(self.nc.semaphore(name))))
        return self.counters[-1]

    def note(self, event, *tokens):
        self.events[event] = list(tokens)

    def upcoming(self, counter, add):
        return Token(counter, counter.count + add, self.loop)

    def value(self, token):
        if token.loop is None:
            return 0, token.value
        step = token.loop.steps.get(token.counter, 0)
        if token.loop is self.loop:
            return step, token.value
        return 0, token.value + (token.loop.n - 1) * step

    def last(self, event):
        now = self.events.get(event, [])
        if self.loop is None or (now and now[0].loop is self.loop):
            return [(t.counter, *self.value(t)) for t in now]
        out = {t.counter: (0, self.value(t)[1]) for t in now}
        for t in self.loop.after.get(event, []):
            if t.loop == "counting":
                step = self.loop.steps[t.counter]
                assert t.value - step > 0, (event, t.value, step)
                out[t.counter] = (step, max(t.value - step, out.get(t.counter, (0, 1))[1]))
        return [(c, m, v) for c, (m, v) in out.items()]

    def repeat(self, n, body):
        start = {c: c.count for c in self.counters}
        before = dict(self.events)
        self.writing, self.loop, seen = False, Loop(n, {}, before, {}), self.loop
        marks = self.loop
        body(0)
        steps = {c: c.count - start[c] for c in self.counters if c.count > start[c]}
        after = {k: [Token(t.counter, t.value, "counting") for t in v] for k, v in self.events.items()
                 if v and v[0].loop is marks}
        for c, v in start.items():
            c.count = v
        self.events = before
        self.writing, self.loop = True, Loop(n, steps, before, after)
        for e in (self.pe, self.act, self.dve, self.pool, self.sp):
            e.seen = {}
        with self.nc.Fori(0, n) as it:
            self.it = it
            body(it)
        for c, step in steps.items():
            assert c.count == start[c] + step
            c.count = start[c] + n * step
        self.loop, self.it = None, 0
        for e in (self.pe, self.act, self.dve, self.pool, self.sp):
            e.seen = {}


class Engine:
    def __init__(self, program, engine, name):
        self.p, self.e, self.seen = program, engine, {}
        self.settle = name in ("act_done", "sp_done")
        self.done = program.counter(name)

    def wait(self, *what):
        waits = []
        for w in what:
            if w is not None:
                waits += self.p.last(w) if isinstance(w, str) else [(w.counter, *self.p.value(w))]
        most = {}
        for c, mult, const in waits:
            most[(c, mult)] = max(const, most.get((c, mult), 0))
        waits = [(c, mult, const) for (c, mult), const in most.items() if self.seen.get((c, mult), 0) < const]
        for c, mult, const in waits:
            self.seen[(c, mult)] = max(const, self.seen.get((c, mult), 0))
        if not self.p.writing:
            return
        waits = [(c, self.e.to_reg(self.p.it * mult + const) if mult and self.settle else
                  self.p.it * mult + const if mult else const, mult) for c, mult, const in waits]
        if self.settle and any(mult for _, _, mult in waits):
            self.e.wait_ge(self.p.always.sem, 16)
        for c, value, _ in waits:
            self.e.wait_ge(c.sem, value)

    def do(self, write, *after, counter=None, add=1):
        self.wait(*after)
        c = counter or self.done
        if self.p.writing:
            write(self.e).then_inc(c.sem, add)
        c.count += add
        return Token(c, c.count, self.p.loop)


ROT1, ROT2 = 16, 64


def const_tables():
    t = {"ident": np.eye(P, dtype=np.float32), "ones": np.ones((P, P), np.float32)}
    p = np.arange(P)
    rot = np.zeros((P, P), np.float32)
    for h in (0, 64):
        for j in range(8):
            rot[h + 8 + j, h + j] = -1.0
            rot[h + j, h + 8 + j] = 1.0
    t["rot1"] = rot
    inv = (np.float32(500000.0) ** (-np.arange(0, ROT1, 2, dtype=np.float32) / np.float32(ROT1))).astype(np.float32)
    freq = np.zeros((P, 1), np.float32)
    for q in range(P):
        if q % 64 < ROT1:
            freq[q, 0] = inv[q % 8]
    t["freq1"] = freq
    rot = np.zeros((P, P), np.float32)
    for h in (0, 64):
        for j in range(32):
            rot[h + 32 + j, h + j] = -1.0
            rot[h + j, h + 32 + j] = 1.0
    t["rot2"] = rot
    inv = (np.float32(10000.0) ** (-np.arange(0, ROT2, 2, dtype=np.float32) / np.float32(ROT2))).astype(np.float32)
    pos = np.arange(S)
    ang = np.zeros((P, T2), np.float32)
    for q in range(P):
        axis = (pos // 64 if q < 64 else pos % 64).astype(np.float32)
        ang[q, :S] = axis * inv[q % 32]
    t["cos2"], t["sin2"] = np.cos(ang).astype(np.float32), np.sin(ang).astype(np.float32)
    qi, kj = np.arange(P)[:, None], np.arange(P)[None, :]
    t["prev"] = np.where(kj > qi, 0.0, -1e30).astype(np.float32)
    t["own"] = np.where(kj <= qi, 0.0, -1e30).astype(np.float32)
    s, u = (p % CH)[:, None], np.arange(CH)[None, :]
    t["diag"] = (s == u).astype(np.float32)
    for m in (32, 16, 8, 4, 2, 1):
        same = (s // (2 * m)) == (u // (2 * m))
        t[f"lvl{m}"] = (same & (s % (2 * m) < m) & (u % (2 * m) >= m)).astype(np.float32)
    t["later"] = (s > u).astype(np.float32)
    at, cols, n = {}, [], 0
    for k, v in t.items():
        at[k] = (n, n + v.shape[1])
        cols.append(v)
        n += v.shape[1]
    return at, np.concatenate(cols, axis=1)


def flat(ap):
    return ap.rearrange("p a b -> p (a b)")


def build(nc, x, c, positions, w_ada, b_ada, g_pre_mix, g_post_mix, g_pre_ffn, g_post_ffn, w_in, attn_sinks,
          w_attn_proj, hg_lower_bounds, hg_norm, w_hgrn_proj, w_out, w_ffn_in, w_ffn_out, meta_tokens_2,
          pre_norm_2, post_norm_2, attn_w_in_2, attn_q_norm_2, attn_k_norm_2, attn_w_out_2, gla_w_in_2,
          gla_gk_up_2, gla_gk_bias_2, gla_o_norm_2, gla_w_out_2, consts, out):
    ctx = ExitStack()
    with ctx:
        k = Kernel(nc, ctx, consts)
        k.gla_w_in, k.gla_up = gla_w_in_2[0], gla_gk_up_2[0]
        k.start(x, c, positions, meta_tokens_2, attn_sinks,
                [[(c, 16), (g_pre_mix, 16), (g_post_mix, 16), (g_pre_ffn, 16), (g_post_ffn, 16),
                  (hg_lower_bounds, 16), (pre_norm_2, 32)],
                 [(post_norm_2, 32), (gla_gk_bias_2, 16), (gla_o_norm_2, 4), (attn_q_norm_2, 1),
                  (attn_k_norm_2, 1), (hg_norm, 1)],
                 [(b_ada, 96)]])
        k.first_block(w_ada[0], w_in[0], w_attn_proj[0], w_hgrn_proj[0], w_out[0], w_ffn_in[0], w_ffn_out[0])
        k.second_block(attn_w_in_2[0], attn_w_out_2[0], gla_w_in_2[0], gla_w_out_2[0])
        k.finish(out)


def columns(w, c0, k0=0, kt=KT, n=256):
    return w[k0 * P:(k0 + kt) * P, bass.ds(c0, n)].rearrange("(k p) n -> p k n", p=P)


class Kernel:
    def __init__(self, nc, ctx, consts):
        self.nc, self.consts = nc, consts
        p = self.p = Program(nc, ctx)
        self.pe, self.act, self.dve, self.pool, self.sp = p.pe, p.act, p.dve, p.pool, p.sp
        self.top = 1152

        def sb(name, shape, dtype=F32, at=None):
            n = 4 * int(np.prod(shape[1:]))
            n += -n % 32
            if at is None:
                at, self.top = self.top, self.top + n
            assert at + n <= 229344, (name, at, n)
            return nc.alloc_sbuf_tensor_at(name, shape, dtype, offset=at)

        self.sb = sb
        self.raw = sb("raw", [P, SLOTS, UNIT])
        self.split_at = self.top
        self.wh = sb("wh", [P, 4, SUB], F32R)
        self.wl = sb("wl", [P, 4, SUB], F32R)
        self.X = sb("X", [P, KT, T2])
        self.ah_at = self.top
        self.ah = sb("ah", [P, KT, T2], F32R)
        self.al = sb("al", [P, KT, T2], F32R)
        self.cat, table = const_tables()
        self.nconst = table.shape[1]
        self.cs = sb("cs", [P, self.nconst + 7])
        self.col = self.cs[:, self.nconst:self.nconst + 7]
        self.vec = sb("vec", [P, 3, P])
        self.mod = sb("mod", [P, 96])
        self.sinks = sb("sinks", [P, 16])
        self.scale1 = sb("scale1", [P, KT])
        self.gate1 = sb("gate1", [P, KT])
        self.work = self.top
        self.acc = sb("acc", [P, 2, 2, 256])
        self.sq = sb("sq", [P, 4, T2])
        self.tmp_at = self.top
        self.tmp, self.tmp2 = sb("tmp", [P, 2, T2]), sb("tmp2", [P, 2, T2])
        self.t4 = sb("t4", [P, 4, T2], at=self.tmp_at)
        self.rs, self.rs2 = sb("rs", [P, T2]), sb("rs2", [P, T2])
        self.big = self.top
        self.bank = ctx.enter_context(nc.psum_tensor("bank", [P, 8, 512], F32))
        self.arrived = [p.counter(f"raw{i}_arrived") for i in range(SLOTS)]
        self.high = p.counter("wh_made")
        self.low = p.counter("wl_made")
        self.used = p.counter("eighth_multiplied")
        self.ada_sum = p.counter("ada_unit_summed")
        self.small_in = p.counter("small_loads")
        self.stored = p.counter("stored")
        self.units = 0
        self.sq_turn = 0
        self.fill_behind = False

    def C(self, name, a=None, b=None):
        lo, hi = self.cat[name]
        lo, hi = (lo, hi) if a is None else (lo + a, lo + b)
        return self.cs[:, lo:hi]

    def load(self, first, second):
        slot = self.units % SLOTS
        self.units += 1
        self.sp.wait(f"raw{slot} read")
        for where, view in (first, second):
            dst = where(self.raw[:, slot, :])
            self.sp.do(lambda e, dst=dst, view=view: e.dma_start(dst, view), counter=self.arrived[slot], add=16)
        return slot

    def load_columns(self, w, c0, k0=0):
        half = lambda i: (lambda r: r.rearrange("p (k n) -> p k n", n=256)[:, 8 * i:8 * i + 8, :],
                          columns(w, c0, k0 + 8 * i, 8))
        return self.load(half(0), half(1))

    def landed(self, slot, pending=False):
        c = self.arrived[slot]
        return self.p.upcoming(c, 32) if pending else Token(c, c.count, self.p.loop)

    def split(self, slot, q, landed):
        src, r = self.raw[:, slot, q * SUB:(q + 1) * SUB], q % 4
        high = self.act.do(lambda e: e.activation(self.wh[:, r, :], src, ACT.Copy),
                           landed, f"w{r} used", counter=self.high)
        low = self.dve.do(lambda e: e.tensor_tensor(self.wl[:, r, :], src, self.wh[:, r, :].bitcast(F32),
                                                    ALU.subtract), high, counter=self.low)
        if q == 7:
            self.p.note(f"raw{slot} read", low)
        self.p.note(f"w{r} split", low)

    def split_first(self):
        for q in range(4):
            self.split(self.units % SLOTS, q, self.landed(self.units % SLOTS, pending=True))

    def unit(self, slot, plan, nxt=None, pending=False, free=(), ready=(), between=None):
        here = self.landed(slot)
        there = None if nxt is None else self.landed(nxt, pending)
        self.pe.wait(*free)
        for q in range(8):
            self.pe.wait(*ready[q:q + 1])

            def products(e, q=q):
                for dst, cols, ah, al, start, stop in plan[q]:
                    wh, wl = cols(self.wh[:, q % 4, :]), cols(self.wl[:, q % 4, :])
                    e.matmul(dst, wh, ah, start=start, stop=False, skip_group_check=True)
                    e.matmul(dst, wh, al, start=False, stop=False, skip_group_check=True)
                    last = e.matmul(dst, wl, ah, start=False, stop=stop, skip_group_check=True)
                return last
            done = self.pe.do(products, f"w{q % 4} split", counter=self.used)
            self.p.note(f"w{q % 4} used", done)
            if between:
                between(q)
            if q < 4:
                self.split(slot, q + 4, here)
            elif nxt is not None:
                self.split(nxt, q - 4, there)
        return done

    def plan(self, outs, T, k0=0, ah=None, al=None):
        ah, al = ah or self.ah, al or self.al

        def cols(kk, j):
            return lambda w: w[:, kk * 256 + j * P:kk * 256 + (j + 1) * P]
        return [[(outs[j], cols(kk, j), ah[:, 2 * q + kk, 0:T], al[:, 2 * q + kk, 0:T],
                  q == 0 and kk == 0, q == 7 and kk == 1) for j in range(2) for kk in range(2)] for q in range(8)]

    def b(self, i, n=T2, lo=0, p=P, p0=0):
        return self.bank[p0:p0 + p, i, lo:lo + n]

    def ada_step(self, slot, turn, q, n=2):
        if q == 0:
            self.dve.wait(self.landed(slot), f"acc{turn} read")
        for kk in range(n * q, n * q + n):
            acc = self.acc[:, turn, kk % 2, :]
            w, ccol = self.raw[:, slot, kk * 256:(kk + 1) * 256], self.vec[:, 0, kk:kk + 1]
            last = dict(counter=self.ada_sum) if kk == KT - 1 else {}
            if kk < 2:
                t = self.dve.do(lambda e: e.tensor_scalar(acc, w, ccol, None, ALU.mult))
            else:
                t = self.dve.do(lambda e: e.scalar_tensor_tensor(out=acc, in0=w, scalar=ccol, in1=acc, op0=ALU.mult,
                                                                 op1=ALU.add), f"chain{kk % 2}", **last)
            self.p.note(f"chain{kk % 2}", t)
            if kk == KT - 2:
                self.even_done = t
            if kk == KT - 1:
                self.p.note(f"raw{slot} read", t)
                self.p.note(f"acc{turn} made", self.even_done, t)

    def ada_columns(self, turn, index):
        def sums(e):
            for j in range(2):
                for ch in range(2):
                    last = e.matmul(self.bank[:, 7, bass.ds(index * 2 + j, 1)], self.acc[:, turn, ch, j * P:(j + 1) * P],
                                    self.C("ones", 0, 1), start=ch == 0, stop=ch == 1, skip_group_check=True)
            return last
        self.p.note(f"acc{turn} read", self.pe.do(sums, f"acc{turn} made", "bank7 read"))

    def fill_start(self, w_ada, first, last):
        self.acc_own, self.acc = self.acc, self.sb("acc_fill", [P, 2, 2, 256], at=self.split_at)
        self.fill_load = lambda n: self.load_columns(w_ada, n * 256)
        self.fill_next, self.fill_last, self.fill_tile = first, last, 0
        self.fill_slots = [self.fill_load(first + i) for i in range(4)]

    def fill(self, n):
        for _ in range(n):
            if self.fill_next == self.fill_last:
                return
            index, turn = self.fill_next, self.fill_next % 2
            self.ada_step(self.fill_slots[0], turn, self.fill_tile, n=1)
            if self.fill_tile == 4 and self.fill_behind:
                self.ada_columns(1 - turn, index - 1)
                self.fill_behind = False
            self.fill_tile += 1
            if self.fill_tile == KT:
                self.fill_tile, self.fill_behind = 0, True
                self.fill_next += 1
                self.fill_slots.pop(0)
                if index + 4 < self.fill_last:
                    self.fill_slots.append(self.fill_load(index + 4))

    def fill_end(self):
        self.fill(16 * (self.fill_last - self.fill_next))
        self.ada_columns((self.fill_last - 1) % 2, self.fill_last - 1)
        self.fill_behind = False
        self.acc = self.acc_own

    def ada_take(self, lo, hi):
        t = self.dve.do(lambda e: e.tensor_tensor(self.mod[:, lo:hi], self.bank[:, 7, lo:hi], self.vec[:, 2, lo:hi],
                                                  ALU.add), "acc0 read", "acc1 read")
        self.p.note("bank7 read", t)
        return t

    def rstd(self, bank, n, width, tile, summed):
        root = self.act.do(lambda e: e.activation(tile, self.b(bank, n), ACT.Sqrt, bias=self.col[:, 0:1],
                                                  scale=1.0 / width), summed)
        self.p.note(f"bank{bank} read", root)
        return self.dve.do(lambda e: e.reciprocal(tile, tile), root)

    def square_into(self, src, n, first, last, after, engine=None):
        t = self.sq_turn = (self.sq_turn + 1) % 4
        sq = self.sq[:, t, 0:n]
        a = self.act.do(lambda e: e.activation(sq, src, ACT.Square), after, f"sq{t} read")
        m = self.pe.do(lambda e: e.matmul(self.b(6, n), self.C("ones"), sq, start=first, stop=last,
                                          skip_group_check=True), a, *(["bank6 read"] if first else []))
        self.p.note(f"sq{t} read", m)
        return m

    def operand(self, n, rs, scale, shift, rs_ready, free=True):
        self.act.wait("operand free")
        self.dve.wait("operand free")
        highs = []

        def low(kt):
            t = self.dve.do(lambda e: e.scalar_tensor_tensor(
                out=self.al[:, kt, 0:n], in0=self.t4[:, kt % 4, 0:n], scalar=shift[:, kt:kt + 1],
                in1=self.ah[:, kt, 0:n].bitcast(F32), op0=ALU.add, op1=ALU.subtract), highs[kt])
            self.p.note(f"t4-{kt % 4} read", t)
            if kt % 2:
                self.p.note(f"operand {kt // 2}", t)
        for kt in range(KT):
            f = self.dve.do(lambda e: e.scalar_tensor_tensor(
                out=self.t4[:, kt % 4, 0:n], in0=self.X[:, kt, 0:n], scalar=scale[:, kt:kt + 1], in1=rs[:, 0:n],
                op0=ALU.mult, op1=ALU.mult), rs_ready, f"t4-{kt % 4} read")
            highs.append(self.act.do(lambda e: e.activation(self.ah[:, kt, 0:n], self.t4[:, kt % 4, 0:n], ACT.Identity,
                                                            bias=shift[:, kt:kt + 1]), f))
            if kt >= 2:
                low(kt - 2)
        low(KT - 2)
        low(KT - 1)

    READY = [f"operand {q}" for q in range(8)]

    def residual(self, n, m_n, y, coef, post_summed, gain=None):
        r = self.rstd(6, n, D, self.rs[:, 0:n], post_summed)
        if gain is not None:
            self.act.wait("operand free")
            self.dve.wait("operand free")
        adds, highs = [], []

        def after(kt):
            m = self.square_into(self.X[:, kt, 0:m_n], m_n, kt == 0, kt == KT - 1, adds[kt])
            if gain is not None:
                highs.append(self.act.do(lambda e: e.activation(self.ah[:, kt, 0:m_n], self.X[:, kt, 0:m_n], ACT.Copy,
                                                                scale=gain[:, kt:kt + 1])))
            return m

        def low(kt):
            t = self.dve.do(lambda e: e.scalar_tensor_tensor(
                out=self.al[:, kt, 0:m_n], in0=self.X[:, kt, 0:m_n], scalar=gain[:, kt:kt + 1],
                in1=self.ah[:, kt, 0:m_n].bitcast(F32), op0=ALU.mult, op1=ALU.subtract), highs[kt])
            if kt % 2:
                self.p.note(f"operand {kt // 2}", t)
        for kt in range(KT):
            tmp = self.t4[:, kt % 4, 0:n]
            f = self.dve.do(lambda e: e.scalar_tensor_tensor(out=tmp, in0=y[:, kt, 0:n], scalar=coef[:, kt:kt + 1],
                                                             in1=self.rs[:, 0:n], op0=ALU.mult, op1=ALU.mult),
                            r, f"t4-{kt % 4} read")
            adds.append(self.pool.do(lambda e: e.tensor_tensor(self.X[:, kt, 0:n], self.X[:, kt, 0:n], tmp, ALU.add), f))
            self.p.note(f"t4-{kt % 4} read", adds[kt])
            m = after(kt)
            if gain is not None and kt >= 3:
                low(kt - 3)
        if gain is not None:
            for kt in range(KT - 3, KT):
                low(kt)
        self.x_done = adds[-1]
        return self.rstd(6, m_n, D, self.rs2[:, 0:m_n], m)

    def join(self):
        engines = (self.pe, self.act, self.dve, self.pool)
        now = [Token(e.done, e.done.count, None) for e in engines if e.done.count]
        now += [Token(c, c.count, None) for c in (self.used,) if c.count]
        for e in engines:
            e.wait(*now)
        return now

    def start(self, x, c, positions, meta, sinks, groups):
        sp, p = self.sp, self.p
        consts_in, rows_in, x_in = p.always, p.counter("rows_in"), p.counter("x_in")
        self.rows = self.sb("rows", [P, 3, P], at=self.big)
        self.xrows = self.sb("xrows", [P, 2, D], at=self.big + 1536)
        self.mrows = self.sb("mrows", [META, D], at=self.big + 1536 + 16384)
        self.pos = self.sb("pos", [P, S], I32, at=self.big + 44000)
        self.angle = self.sb("angle", [P, 2, S], at=self.big + 45024)

        sp.do(lambda e: e.dma_start(self.cs[:, 0:self.nconst], self.consts), counter=consts_in, add=16)
        for g, group in enumerate(groups):
            at = 0
            for ap, n in group:
                dims = " ".join("abc"[:len(ap.shape) - 1])
                view = ap.rearrange(f"{dims} (j p) -> ({dims} j) p", p=P) if len(ap.shape) > 1 else ap
                sp.do(lambda e, view=view, at=at, n=n, g=g: e.dma_start(self.rows[at:at + n, g, :], view),
                      counter=rows_in, add=16)
                at += n
        sp.do(lambda e: e.dma_start(self.xrows[:, :, :], x[0].rearrange("(i p) d -> p i d", p=P)), counter=x_in, add=16)
        sp.do(lambda e: e.dma_start(self.mrows[:, :], meta), counter=x_in, add=16)
        sp.do(lambda e: e.dma_start(self.pos[:, :], positions.to_broadcast([P, S])), counter=x_in, add=16)
        sp.do(lambda e: e.dma_start(self.sinks[:, :], sinks.to_broadcast([P, 16])), counter=x_in, add=16)
        consts, rows, xs = (Token(q, q.count, None) for q in (consts_in, rows_in, x_in))
        self.dve.do(lambda e: e.memset(self.col[:, 4:5], 0.0), counter=self.ada_sum, add=4)
        self.dve.do(lambda e: e.memset(self.col[:, 0:1], EPS))
        cols = self.dve.do(lambda e: e.memset(self.col[:, 1:2], 1.0))
        self.pool.wait(cols)
        self.act.wait(cols)
        for e in (self.pe, self.act, self.dve, self.pool):
            e.wait(consts, rows, xs)

        ang, turns = self.angle[:, 0, :], self.angle[:, 1, :]
        self.cos1, self.sin1 = self.angle[:, 0, :], self.angle[:, 1, :]
        two_pi = 2 * np.pi
        c1 = 6.28125
        c2 = float(np.float32(two_pi - c1).view(np.uint32) & np.uint32(0xFFFFF000))
        c2 = float(np.array(int(c2), np.uint32).view(np.float32))
        c3 = two_pi - c1 - c2
        dve = self.dve
        t = dve.do(lambda e: e.tensor_copy(ang, self.pos[:, :]))
        t = dve.do(lambda e: e.tensor_scalar(ang, ang, self.C("freq1"), None, ALU.mult), t)
        t = dve.do(lambda e: e.tensor_scalar(turns, ang, float(1 / two_pi), 12582912.0, ALU.mult, ALU.add), t)
        t = dve.do(lambda e: e.tensor_scalar(turns, turns, 12582912.0, None, ALU.subtract), t)
        for part in (c1, c2, c3):
            t = dve.do(lambda e: e.scalar_tensor_tensor(out=ang, in0=turns, scalar=-float(part), in1=ang, op0=ALU.mult,
                                                        op1=ALU.add), t)
        t = dve.do(lambda e: e.tensor_scalar(ang, ang, 3.1415925, -3.1415925, ALU.min, ALU.max), t)
        t = self.act.do(lambda e: e.activation(self.sin1, ang, ACT.Sin), t)
        t = self.act.do(lambda e: e.activation(self.cos1, ang, ACT.Sin, scale=0.5), t)
        t = dve.do(lambda e: e.tensor_tensor(self.cos1, self.cos1, self.cos1, ALU.mult), t)
        self.trig = dve.do(lambda e: e.tensor_scalar(self.cos1, self.cos1, -2.0, 1.0, ALU.mult, ALU.add), t)

        def vec_rows(e):
            for g, n in enumerate((128, 55, 96)):
                last = e.transpose(self.b(0, n, g * P), self.rows[0:n, g, :], self.cs[0:n, self.cat["ident"][0]:
                                                                                self.cat["ident"][0] + n])
            return last
        t = self.pe.do(vec_rows)
        for g, n in enumerate((128, 55, 96)):
            self.vec_done = self.act.do(lambda e: e.activation(self.vec[:, g, 0:n], self.b(0, n, g * P), ACT.Copy), t)
        p.note("bank0 read", self.vec_done)
        self.dve.wait(self.vec_done)
        self.pe.wait(self.vec_done)
        for n, (i, g) in enumerate((i, g) for i in range(2) for g in range(4)):
            bank = 1 + n % 4

            def turn(e):
                for j in range(4):
                    last = e.transpose(self.b(bank, P, j * P), self.xrows[:, i, (4 * g + j) * P:(4 * g + j + 1) * P],
                                       self.C("ident"))
                return last
            t = self.pe.do(turn, f"bank{bank} read")
            t = self.act.do(lambda e: e.activation(self.X[:, 4 * g:4 * g + 4, i * P:(i + 1) * P],
                                                   self.b(bank, 512).rearrange("p (k n) -> p k n", k=4), ACT.Copy), t)
            p.note(f"bank{bank} read", t)

        def turn_meta(e):
            for j in range(KT):
                last = e.transpose(self.b(5, META, j * META), self.mrows[:, j * P:(j + 1) * P],
                                   self.cs[0:META, self.cat["ident"][0]:self.cat["ident"][0] + META])
            return last
        t = self.pe.do(turn_meta)
        t = self.x_done = self.act.do(lambda e: e.activation(
            self.X[:, :, S:T2], self.b(5, 256).rearrange("p (k n) -> p k n", k=KT), ACT.Copy), t)
        self.wlr = self.sb("wlr", [P, KT, 48], at=self.big + 57344)
        self.low_in = p.counter("low_rank_in")
        self.wlr_zero = self.pool.do(lambda e: e.memset(self.wlr[:, :, 16:32], 0.0))
        for d in range(2):
            sp.do(lambda e: e.dma_start(self.wlr[:, :, 32 * d:32 * d + 16], columns(self.gla_w_in, 6144 + 16 * d, n=16)),
                  counter=self.low_in, add=16)

    def first_block(self, w_ada, w_in, w_ap, w_hp, w_out, w_fi, w_fo):
        p, pe, act, dve = self.p, self.pe, self.act, self.dve
        cols = lambda g, n=16: self.vec[:, 0, g:g + n]
        self.pe.do(lambda e: e.matmul(self.b(7, 4), self.C("ones"), self.C("ones", 0, 4), start=True, stop=True),
                   counter=self.used, add=32)
        self.dve.do(lambda e: e.memset(self.col[:, 2:3], 0.0), counter=self.low, add=32)
        self.act.do(lambda e: e.activation(self.col[:, 3:4], self.col[:, 0:1], ACT.Copy), counter=self.high, add=32)

        for kt in range(KT):
            m = self.square_into(self.X[:, kt, 0:S], S, kt == 0, kt == KT - 1, self.x_done)

        def ada_body(it):
            slots = [self.load_columns(w_ada, (it * 4 + j) * 256) for j in range(4)]
            for j, slot in enumerate(slots):
                for q in range(8):
                    self.ada_step(slot, j % 2, q)
                self.ada_columns(j % 2, it * 4 + j)
        p.repeat(4, ada_body)
        rs = self.rstd(6, S, D, self.rs[:, 0:S], m)
        t = self.ada_take(0, 32)
        t = dve.do(lambda e: e.tensor_scalar(self.scale1[:, :], self.mod[:, 16:32], 1.0, None, ALU.add), t)
        t = dve.do(lambda e: e.tensor_tensor(self.scale1[:, :], self.scale1[:, :], cols(16), ALU.mult), t)
        dve.wait(t)
        self.join()
        self.operand(S, self.rs, self.scale1, self.mod[:, 0:16], rs)

        proj = self.proj = self.sb("proj1", [P, 42, S], at=self.big)

        def evict(dst, banks, done, n=S):
            for j in range(2):
                t = act.do(lambda e, j=j: e.activation(dst(j), self.b(banks[j], n), ACT.Copy), done)
                p.note(f"bank{banks[j]} read", t)
            return t

        def w_in_body(it, end=False):
            slots = [self.load_columns(w_in, (it * 3 + j) * 256) for j in range(3)]
            slots.append(self.load_columns(w_ada, (it + 16) * 256))
            for j in range(3):
                banks = (2 * j, 2 * j + 1)
                done = self.unit(slots[j], self.plan([self.b(i, S) for i in banks], S),
                                 None if end and j == 2 else slots[(j + 1) % 3], pending=j == 2,
                                 free=[f"bank{i} read" for i in banks], ready=self.READY,
                                 between=(lambda q: self.ada_step(slots[3], 0, q + 8 * j - 8, n=1)) if j else None)
                evict(lambda i: flat(proj[:, bass.ds((it * 3 + j) * 2 + i, 1), :]), banks, done)
            self.ada_columns(0, it + 16)
        self.split_first()
        p.repeat(6, w_in_body)
        w_in_body(6, end=True)
        self.ada_take(32, 46)
        self.join()
        self.fill_start(w_ada, 23, 36)
        self.attention1()
        self.join()
        self.hgrn()
        self.fill_end()
        self.ada_take(46, 72)
        self.join()
        self.split_first()
        self.merge(w_in, w_ap, w_hp, w_ada)
        self.ada_take(72, 88)

        t = dve.do(lambda e: e.tensor_tensor(self.gate1[:, :], self.mod[:, 32:48], cols(32), ALU.mult))
        t = dve.do(lambda e: e.tensor_scalar(self.scale1[:, :], self.mod[:, 64:80], 1.0, None, ALU.add), t)
        t = dve.do(lambda e: e.tensor_tensor(self.scale1[:, :], self.scale1[:, :], cols(48), ALU.mult), t)
        dve.wait(t)
        y = self.y = self.sb("y", [P, KT, T2], at=self.big + 32768)
        summed = self.to_y(w_out, S)
        rs = self.residual(S, S, y, self.gate1, summed)
        self.operand(S, self.rs2, self.scale1, self.mod[:, 48:64], rs)

        summed = self.feed_forward(w_fi, w_fo, w_ada)
        self.up = self.sb("up", [48, 1024], at=self.work)
        for d in range(2):
            self.sp.do(lambda e: e.dma_start(self.up[32 * d:32 * d + 16, :], self.gla_up[d]), "acc0 read", "acc1 read",
                       counter=self.low_in, add=16)
        t = dve.do(lambda e: e.tensor_tensor(self.gate1[:, :], self.mod[:, 80:96], cols(64), ALU.mult))
        dve.wait(t)
        self.rs2_done = self.residual(S, T2, y, self.gate1, summed, gain=self.vec[:, 0, 96:112])

    def merge(self, w_in, w_ap, w_hp, w_ada):
        p, pe, act, dve, pool, proj = self.p, self.pe, self.act, self.dve, self.pool, self.proj
        at = self.big + 18432
        parts = [self.sb(n, [P, 8, S], F32R, at=at + 8192 * i) for i, n in enumerate(("oah", "oal", "ohh", "ohl"))]
        merged = self.sb("merged", [P, KT, S], at=self.big)
        for i, t0 in enumerate((0, 10)):
            h, l = parts[2 * i], parts[2 * i + 1]
            src = flat(proj[:, t0:t0 + 8, :])
            t = act.do(lambda e: e.activation(flat(h[:, :, :]), src, ACT.Copy))
            t = dve.do(lambda e: e.tensor_tensor(flat(l[:, :, :]), src, flat(h[:, :, :]).bitcast(F32), ALU.subtract), t)
        p.note("parts made", t)

        def body(it):
            col = it * 256
            half = lambda w, i: (lambda r: r.rearrange("p (k n) -> p k n", n=256)[:, 8 * i:8 * i + 8, :],
                                 columns(w, col, 0, 8))
            slots = [self.load_columns(w_in, col + 21 * 256), self.load_columns(w_in, col + 29 * 256),
                     self.load(half(w_ap, 0), half(w_hp, 1)), self.load_columns(w_ada, (it + 36) * 256)]
            for i in range(2):
                sg = (self.tmp, self.tmp2)[i]
                banks = (2 * i, 2 * i + 1)
                done = self.unit(slots[i], self.plan([self.b(j, S) for j in banks], S), slots[i + 1],
                                 free=[f"bank{j} read" for j in banks],
                                 between=(lambda q: self.ada_step(slots[3], 0, q, n=1)) if i else None)
                for j in range(2):
                    t = act.do(lambda e: e.activation(sg[:, j, 0:S], self.b(banks[j], S), ACT.Sigmoid), done,
                               f"sg{i} read")
                    p.note(f"bank{banks[j]} read", t)
                p.note(f"sg{i} made", t)

            def cols(kk, j):
                return lambda w: w[:, kk * 256 + j * P:kk * 256 + (j + 1) * P]
            plan = [[(self.b(4 + j, S, (q // 4) * S), cols(kk, j), parts[2 * (q // 4)][:, 2 * (q % 4) + kk, :],
                      parts[2 * (q // 4) + 1][:, 2 * (q % 4) + kk, :], q % 4 == 0 and kk == 0, q % 4 == 3 and kk == 1)
                     for j in range(2) for kk in range(2)] for q in range(8)]
            done = self.unit(slots[2], plan, slots[0], pending=True, free=["bank4 read", "bank5 read"],
                             ready=["parts made"],
                             between=lambda q: self.ada_step(slots[3], 0, q + 8, n=1))
            self.ada_columns(0, it + 36)
            for i in range(2):
                sg = (self.tmp, self.tmp2)[i]
                ps = self.bank[:, 4:6, i * S:(i + 1) * S]
                t = dve.do(lambda e: e.tensor_tensor(sg[:, :, 0:S], sg[:, :, 0:S], ps, ALU.mult), done, f"sg{i} made")
            p.note("bank4 read", t)
            p.note("bank5 read", t)
            t = pool.do(lambda e: e.tensor_tensor(merged[:, bass.ds(it * 2, 2), :], self.tmp[:, :, 0:S],
                                                  self.tmp2[:, :, 0:S], ALU.add), t)
            p.note("sg0 read", t)
            p.note("sg1 read", t)
        p.repeat(8, body)
        self.join()
        for kt in range(KT):
            h = act.do(lambda e: e.activation(self.ah[:, kt, 0:S], merged[:, kt, :], ACT.Copy))
            t = dve.do(lambda e: e.tensor_tensor(self.al[:, kt, 0:S], merged[:, kt, :],
                                                 self.ah[:, kt, 0:S].bitcast(F32), ALU.subtract), h)
            if kt % 2:
                p.note(f"operand {kt // 2}", t)

    def to_y(self, w, n, last=False):
        p, pe, act, dve, y = self.p, self.pe, self.act, self.dve, self.y
        z = dve.do(lambda e: e.memset(self.sq[:, :, :], 0.0), *[f"sq{i} read" for i in range(4)])
        p.note("squares1 made", z)
        pe.do(lambda e: e.matmul(self.b(6, n), self.C("ones"), self.sq[:, 0, 0:n], start=True, stop=False,
                                 skip_group_check=True), z, "bank6 read")

        def add_squares(turn, stop=False):
            def products(e):
                for j in range(2):
                    last = e.matmul(self.b(6, n), self.C("ones"), self.sq[:, 2 * turn + j, 0:n], start=False,
                                    stop=stop and j == 1, skip_group_check=True)
                return last
            t = pe.do(products, f"squares{turn} made")
            p.note(f"squares{turn} read", t)
            return t

        def body(it, end=False):
            slots = [self.load_columns(w, (it * 4 + j) * 256) for j in range(4)]
            for j in range(4):
                turn = j % 2
                banks = (2 * turn, 2 * turn + 1)
                nxt = None if end and j == 3 else slots[(j + 1) % 4]
                done = self.unit(slots[j], self.plan([self.b(i, n) for i in banks], n), nxt, pending=j == 3,
                                 free=[f"bank{i} read" for i in banks], ready=self.READY)
                add_squares(1 - turn)
                for i in range(2):
                    act.do(lambda e: e.activation(flat(y[:, bass.ds((it * 4 + j) * 2 + i, 1), 0:n]),
                                                  self.b(banks[i], n), ACT.Copy), done)
                    t = act.do(lambda e: e.activation(self.sq[:, 2 * turn + i, 0:n], self.b(banks[i], n), ACT.Square),
                               f"squares{turn} read")
                    p.note(f"bank{banks[i]} read", t)
                p.note(f"squares{turn} made", t)
            p.note("operand free", done)
        if last:
            body(0)
            body(1, end=True)
        else:
            p.repeat(2, body)
        t = add_squares(1, stop=True)
        for i in range(4):
            p.note(f"sq{i} read", t)
        return t

    def feed_forward(self, w_fi, w_fo, w_ada):
        p, pe, act, dve, y = self.p, self.pe, self.act, self.dve, self.y
        fh = self.sb("fh", [P, KT, S], F32R, at=self.big)
        fl = self.sb("fl", [P, KT, S], F32R, at=self.big + 16384)

        def hidden_load(tile):
            half = lambda i: (lambda r: r.rearrange("p (k n) -> p k n", n=256)[:, :, i * P:(i + 1) * P],
                              columns(w_fi, tile * P + i * FFN, n=P))
            return self.load(half(0), half(1))

        def hidden(slot, nxt, pending, turn, dst, between=None):
            banks = (2 * turn, 2 * turn + 1)
            done = self.unit(slot, self.plan([self.b(i, S) for i in banks], S), nxt, pending,
                             free=[f"bank{i} read" for i in banks], ready=self.READY, between=between)
            b = turn % 2
            g, full = self.tmp[:, b, 0:S], self.tmp2[:, b, 0:S]
            a = act.do(lambda e: e.activation(g, self.b(banks[0], S), ACT.Silu), done, f"silu{b} read")
            p.note(f"bank{banks[0]} read", a)
            t = dve.do(lambda e: e.tensor_tensor(full, g, self.b(banks[1], S), ALU.mult), a)
            p.note(f"bank{banks[1]} read", t)
            p.note(f"silu{b} read", t)
            high, low = flat(fh[:, bass.ds(dst, 1), :]), flat(fl[:, bass.ds(dst, 1), :])
            t = dve.do(lambda e: e.tensor_copy(high, full), t, "hidden free")
            t = dve.do(lambda e: e.tensor_tensor(low, full, high.bitcast(F32), ALU.subtract), t)
            p.note("hidden made", t)

        for part in range(2):
            def in_body(it):
                slots = [hidden_load(it * 4 + j + 16 * part) for j in range(4)]
                for j in range(4):
                    hidden(slots[j], slots[(j + 1) % 4], j == 3, j % 2, it * 4 + j)
            p.repeat(4, in_body)

            def out_body(it):
                slots = [self.load_columns(w_fo, (it * 4 + j) * 256, 16 * part) for j in range(4)]
                for j in range(4):
                    banks = (2 * (j % 2), 2 * (j % 2) + 1)
                    done = self.unit(slots[j], self.plan([self.b(i, S) for i in banks], S, ah=fh, al=fl),
                                     slots[(j + 1) % 4], j == 3, free=[f"bank{i} read" for i in banks],
                                     ready=["hidden made"])
                    for i in range(2):
                        dst = flat(y[:, bass.ds((it * 4 + j) * 2 + i, 1), 0:S])
                        if part == 0:
                            t = act.do(lambda e: e.activation(dst, self.b(banks[i], S), ACT.Copy), done)
                        else:
                            t = dve.do(lambda e: e.tensor_tensor(dst, dst, self.b(banks[i], S), ALU.add), done)
                        p.note(f"bank{banks[i]} read", t)
                p.note("hidden free", done)
            p.repeat(2, out_body)
            if part == 0:
                dve.wait(Token(act.done, act.done.count, None))

        def last_body(it):
            slots = [hidden_load(it * 3 + j + 32) for j in range(3)] + [self.load_columns(w_ada, (it + 44) * 256)]
            for j in range(3):
                between = (lambda q: self.ada_step(slots[3], 0, q + 8 * j - 8, n=1)) if j else None
                hidden(slots[j], slots[(j + 1) % 3], j == 2, j, it * 3 + j, between=between)
            self.ada_columns(0, it + 44)
        p.repeat(4, last_body)
        p.note("operand free", Token(self.used, self.used.count, None))
        self.ada_take(88, 96)
        at = lambda blk, j: self.b(2 * (blk % 2) + j // 2, S, (j % 2) * S)
        added = []

        def block_load(u):
            def half(i):
                h = 2 * u + i
                k0, c0 = 32 + 4 * (h % 3), 512 * (h // 3)
                return (lambda r: r[:, i * 2048:(i + 1) * 2048].rearrange("p (k n) -> p k n", n=512),
                        columns(w_fo, c0, k0, 4, 512))
            return self.load(half(0), half(1))
        slots = [block_load(u) for u in range(4)]
        after = (self.units + 2) % SLOTS
        for u in range(6):
            plan, free = [], []
            for q in range(8):
                e8 = 8 * u + q
                blk, kt = e8 // 12, e8 % 12
                if kt == 0:
                    free += [f"bank{2 * (blk % 2) + j} read" for j in range(2)]
                plan.append([(at(blk, j), (lambda j: lambda w: w[:, j * P:(j + 1) * P])(j), fh[:, kt, :],
                              fl[:, kt, :], kt == 0 and j % 2 == 0, kt == 11) for j in range(4)])
            done = self.unit(slots[u], plan, slots[u + 1] if u < 5 else after, pending=u == 5, free=free,
                             ready=["hidden made"])
            if u < 2:
                slots.append(block_load(u + 4))
            for kt, t in added:
                self.square_into(y[:, kt, 0:S], S, kt == 0, False, t)
            added = []
            for blk in range(4):
                if (12 * blk + 11) // 8 == u:
                    for j in range(4):
                        dst = y[:, 4 * blk + j, 0:S]
                        t = dve.do(lambda e: e.tensor_tensor(dst, dst, at(blk, j), ALU.add), done)
                        p.note(f"bank{2 * (blk % 2) + j // 2} read", t)
                        added.append((4 * blk + j, t))
        for kt, t in added:
            m = self.square_into(y[:, kt, 0:S], S, False, kt == KT - 1, t)
        return m

    def attention1(self):
        p, pe, act, dve, pool, proj = self.p, self.pe, self.act, self.dve, self.pool, self.proj
        a0 = self.big + 47104
        kd = self.sb("kd", [P, 2, 2, S], at=a0)
        vt = proj[:, 8, :].rearrange("p (i d) -> p i d", i=2)
        pt = self.sb("pt1", [P, 4, 384], at=a0 + 4096)
        pm = self.sb("pm1", [P, 2, 4, 384], at=self.work)
        st = self.sb("st1", [P, 2, 6, 8], at=self.work + 12288)
        bcast = lambda ap, n: ap.unsqueeze(1).broadcast_to([P, n, S])
        turned = None
        for n, t0 in enumerate((8, 0, 2, 4, 6)):
            w = 1 if t0 == 8 else 2
            bank = 5 + n % 2
            self.fill(4)
            xs = proj[:, t0:t0 + w, :]
            ps = self.b(bank, w * S).rearrange("p (a b) -> p a b", a=w)
            r = pe.do(lambda e: e.matmul(self.b(bank, w * S), self.C("rot1"), flat(xs), start=True, stop=True),
                      f"bank{bank} read", self.trig)
            tmp = pm[:, n % 2, 0:2, 0:S][:, 0:w, :]
            s = dve.do(lambda e: e.tensor_tensor(tmp, ps, bcast(self.sin1, w), ALU.mult), r, f"rope{n % 2}")
            p.note(f"bank{bank} read", s)
            q = pool.do(lambda e: e.tensor_tensor(xs, xs, bcast(self.cos1, w), ALU.mult), r, self.trig)
            turned = dve.do(lambda e: e.tensor_tensor(xs, xs, tmp, ALU.add), s, q)
            p.note(f"rope{n % 2}", turned)
            if t0 == 8:
                k_done = turned
        kd_zero = pool.do(lambda e: e.memset(kd[:, :, :, :], 0.0))
        for kv in range(2):
            for half in range(2):
                act.do(lambda e: e.activation(kd[64 * half:64 * half + 64, kv, half, :],
                                              proj[64 * kv:64 * kv + 64, 8, :], ACT.Copy), k_done, kd_zero)
        kd_done = Token(act.done, act.done.count, None)

        def v_turn(e):
            for i in range(2):
                last = e.transpose(self.b(4, P, i * P), proj[:, 9, i * P:(i + 1) * P], self.C("ident"))
            return last
        t = pe.do(v_turn)
        v_done = act.do(lambda e: e.activation(flat(vt), self.b(4, 2 * P), ACT.Copy), t, kd_done)
        p.note("bank4 read", v_done)
        pe.wait(turned, kd_done, v_done)
        scale = 64 ** -0.5
        span = lambda u: (3 * u, 3 * u + 3)

        def scores(g):
            u, kv = g % 2, g // 2
            lo = 3 * u

            def products(e):
                for h in range(4):
                    q = lambda blk: proj[:, (4 * g + h) // 2, blk * P:(blk + 1) * P]
                    e.matmul(self.b(lo, P, h * P), q(0), kd[:, kv, h % 2, 0:P], start=True, stop=True)
                    last = e.matmul(self.b(lo + 1 + h // 2, S, (h % 2) * S), q(1), kd[:, kv, h % 2, :],
                                    start=True, stop=True)
                return last
            t = pe.do(products, *[f"bank{i} read" for i in range(lo, lo + 3)])
            own = self.C("own").unsqueeze(1).broadcast_to([P, 4, P])
            both = self.cs[:, self.cat["prev"][0]:self.cat["own"][1]].unsqueeze(1).broadcast_to([P, 4, S])
            near, far = pm[:, u, :, 0:P], pm[:, u, :, P:384]
            a = dve.do(lambda e: e.scalar_tensor_tensor(
                out=near, in0=self.b(lo, 512).rearrange("p (h k) -> p h k", h=4), scalar=scale, in1=own, op0=ALU.mult,
                op1=ALU.add), t, f"pm{u} read")
            b = dve.do(lambda e: e.scalar_tensor_tensor(
                out=far, in0=self.bank[:, lo + 1:lo + 3, :].rearrange("p a (h k) -> p (a h) k", h=2), scalar=scale,
                in1=both, op0=ALU.mult, op1=ALU.add), t)
            for i in range(lo, lo + 3):
                p.note(f"bank{i} read", b)
            mx, neg, sums, es, den = (st[:, u, i, :] for i in range(5))
            dve.do(lambda e: e.tensor_reduce(mx[:, 0:4], near, AX.X, ALU.max), a)
            t = dve.do(lambda e: e.tensor_reduce(mx[:, 4:8], far, AX.X, ALU.max), b)
            sink = self.sinks[:, 4 * g:4 * g + 4].unsqueeze(1).broadcast_to([P, 2, 4])
            two = lambda ap: ap.rearrange("p (b h) -> p b h", b=2)
            t = dve.do(lambda e: e.tensor_tensor(two(mx), two(mx), sink, ALU.max), t)
            t = dve.do(lambda e: e.tensor_scalar(neg, mx, -1.0, None, ALU.mult), t)
            d = dve.do(lambda e: e.tensor_tensor(two(es), two(neg), sink, ALU.add), t)
            for h in range(4):
                act.do(lambda e: e.activation(pm[:, u, h, 0:P], pm[:, u, h, 0:P], ACT.Exp, bias=neg[:, h:h + 1],
                                              accum_out=sums[:, h:h + 1]), d)
                act.do(lambda e: e.activation(pm[:, u, h, P:384], pm[:, u, h, P:384], ACT.Exp,
                                              bias=neg[:, 4 + h:5 + h], accum_out=sums[:, 4 + h:5 + h]))
            self.fill(16)
            t = act.do(lambda e: e.activation(es, es, ACT.Exp))
            t = dve.do(lambda e: e.tensor_tensor(den, sums, es, ALU.add), t)
            t = dve.do(lambda e: e.reciprocal(den, den), t)
            over = lambda lo, n: den[:, lo:lo + 4].unsqueeze(2).broadcast_to([P, 4, n])
            pool.do(lambda e: e.tensor_tensor(near, near, over(0, P), ALU.mult), t)
            return pool.do(lambda e: e.tensor_tensor(far, far, over(4, S), ALU.mult))

        def values(g, weights):
            u, kv = g % 2, g // 2
            lo = 3 * u

            def turn(e):
                for h in range(4):
                    for j in range(3):
                        n = 3 * h + j
                        last = e.transpose(self.b(lo + n // 4, P, (n % 4) * P), pm[:, u, h, j * P:(j + 1) * P],
                                           self.C("ident"))
                return last
            t = pe.do(turn, weights, *[f"bank{i} read" for i in range(lo, lo + 3)])
            p.note(f"pm{u} read", t)
            t = act.do(lambda e: e.activation(flat(pt[:, :, :]), self.bank[:, lo:lo + 3, :].rearrange("p a b -> p (a b)"),
                                              ACT.Copy), t, "pt read")
            for i in range(lo, lo + 3):
                p.note(f"bank{i} read", t)

            def products(e):
                for h in range(4):
                    po = 64 * (h % 2)
                    v = lambda blk: vt[:, blk, kv * 64:kv * 64 + 64]
                    o = lambda blk: self.b(6, P, (h // 2) * S + blk * P, p=64, p0=po)
                    e.matmul(o(0), v(0), pt[:, h, 0:P], start=True, stop=True, skip_group_check=True)
                    e.matmul(o(1), v(0), pt[:, h, P:2 * P], start=True, stop=False, skip_group_check=True)
                    last = e.matmul(o(1), v(1), pt[:, h, 2 * P:3 * P], start=False, stop=True, skip_group_check=True)
                return last
            t = pe.do(products, t, "bank6 read")
            p.note("pt read", t)
            t = act.do(lambda e: e.activation(flat(proj[:, 2 * g:2 * g + 2, :]), self.b(6, 512), ACT.Copy), t)
            p.note("bank6 read", t)

        ready = scores(0)
        for g in range(1, 4):
            nxt = scores(g)
            values(g - 1, ready)
            ready = nxt
        values(3, ready)

    def hgrn(self):
        p, pe, act, dve, pool, proj = self.p, self.pe, self.act, self.dve, self.pool, self.proj
        N = 4 * S
        qk = self.sb("qk", [P, 2, N], at=self.work)
        qx = self.sb("qx", [P, 4, 6, CH], at=self.work + 8192)
        a0 = self.big + 43008
        b = self.sb("b", [P, N], at=a0)
        comp = self.sb("comp", [P, 8, CH], at=a0 + 4096)
        sc = self.sb("sc", [P, 4, 384], at=a0 + 6144)
        lb = self.sb("lb", [P, 3, 8], at=self.work + 14336)
        mask = proj[:, 8, :]
        d = dve.do(lambda e: e.tensor_tensor(lb[:, 2, :], self.vec[:, 0, 80:88], self.vec[:, 0, 88:96], ALU.subtract))
        low = act.do(lambda e: e.activation(lb[:, 0, :], lb[:, 2, :], ACT.Sigmoid), d)
        act.do(lambda e: e.activation(flat(proj[:, 18:26, :]), flat(proj[:, 18:26, :]), ACT.Sigmoid))
        sig = act.do(lambda e: e.activation(flat(proj[:, 34:42, :]), flat(proj[:, 34:42, :]), ACT.Sigmoid))
        q_done = act.do(lambda e: e.activation(flat(proj[:, 10:18, :]), flat(proj[:, 10:18, :]), ACT.Silu))
        om = dve.do(lambda e: e.tensor_scalar(lb[:, 1, :], lb[:, 0, :], -1.0, 1.0, ALU.mult, ALU.add), low)
        t = pool.do(lambda e: e.memset(mask, 1.0))
        mask_done = pool.do(lambda e: e.memset(mask.rearrange("p (c n) -> p c n", n=CH)[:, :, 0:1], 0.0), t)
        for h in range(8):
            f = dve.do(lambda e: e.tensor_scalar(proj[:, 18 + h, :], proj[:, 18 + h, :], lb[:, 1, h:h + 1],
                                                 lb[:, 0, h:h + 1], ALU.mult, ALU.add), om, sig)
        for bk in range(4):
            def turn(e):
                for j in range(4):
                    h, i = 2 * bk + j // 2, j % 2
                    last = e.transpose(self.b(bk, P, j * P), proj[:, 26 + h, i * P:(i + 1) * P], self.C("ident"))
                return last
            t = pe.do(turn, f"bank{bk} read")
            t = act.do(lambda e: e.activation(flat(proj[:, 26 + 2 * bk:28 + 2 * bk, :]), self.b(bk, 512), ACT.Copy), t)
            p.note(f"bank{bk} read", t)
        v_done = t
        for hf in range(2):
            heads = [4 * hf + i for i in range(4)]
            q, key = flat(proj[:, 10 + 4 * hf:14 + 4 * hf, :]), flat(proj[:, 18 + 4 * hf:22 + 4 * hf, :])
            t = act.do(lambda e: e.activation(b[:, :], key, ACT.Ln), f, "b read")
            k_done = dve.do(lambda e: e.tensor_scalar(key, key, -1.0, 1.0, ALU.mult, ALU.add), t)
            for h in range(4):
                bh = b[:, h * S:(h + 1) * S]
                scan = dve.do(lambda e: e.tensor_tensor_scan(bh, mask, bh, 0.0, ALU.mult, ALU.add), t, mask_done)
            zero = pool.do(lambda e: e.memset(comp[:, :, :], 0.0), "comp read")
            pe.wait(k_done, q_done)

            def blocks(left, right, bank):
                def products(e):
                    for h in range(4):
                        for ch in range(NCH):
                            lo = h * S + ch * CH
                            last = e.matmul(self.b(bank, CH, (2 * h + ch // 2) * CH, p=CH, p0=CH * (ch % 2)),
                                            left[:, lo:lo + CH], right[:, lo:lo + CH], start=True, stop=True,
                                            skip_group_check=True)
                    return last
                return products
            def select(name, bank, products_done):
                lvl = self.C(name).bitcast(U32).unsqueeze(1).broadcast_to([P, 8, CH])
                t = dve.do(lambda e: e.copy_predicated(comp[:, :, :], lvl,
                                                       self.b(bank, 512).rearrange("p (a t) -> p a t", t=CH)),
                           products_done, zero)
                p.note(f"bank{bank} read", t)
                return t
            waiting = None
            for li, m in enumerate((0, 32, 16, 8, 4, 2, 1)):
                bank = 2 * hf + li % 2
                if m == 0:
                    t = pe.do(blocks(key, q, bank), f"bank{bank} read")
                    name = "diag"
                else:
                    u, name = li % 2, f"lvl{m}"
                    buf = qk[:, u, :]
                    view = lambda ap: ap.rearrange("p (n t) -> p n t", t=2 * m)
                    mid = view(b[:, :])[:, :, m - 1:m].broadcast_to([P, N // (2 * m), 2 * m])
                    t = pool.do(lambda e: e.tensor_tensor(view(buf), view(b[:, :]), mid, ALU.subtract), scan,
                                f"qk{u} read")
                    left, right = view(buf)[:, :, 0:m], view(buf)[:, :, m:2 * m]
                    act.do(lambda e: e.activation(left, left, ACT.Exp, scale=-1.0), t)
                    t = act.do(lambda e: e.activation(right, right, ACT.Exp))
                    dve.do(lambda e: e.tensor_tensor(left, left, view(key)[:, :, 0:m], ALU.mult), t)
                    t = dve.do(lambda e: e.tensor_tensor(right, right, view(q)[:, :, m:2 * m], ALU.mult), q_done)
                    t = pe.do(blocks(buf, buf, bank), t, f"bank{bank} read")
                    p.note(f"qk{u} read", t)
                if waiting:
                    select(*waiting)
                    self.fill(9)
                waiting = (name, bank, t)
            t = select(*waiting)
            comp_done = t
            eb, kend = qk[:, 0, :], qk[:, 1, :]
            chunks = lambda ap: ap.rearrange("p (n t) -> p n t", t=CH)
            t = pool.do(lambda e: e.tensor_tensor(chunks(kend), chunks(b[:, :])[:, :, CH - 1:CH].broadcast_to([P, 16, CH]),
                                                  chunks(b[:, :]), ALU.subtract), "qk1 read")
            e1 = act.do(lambda e: e.activation(eb, b[:, :], ACT.Exp), "qk0 read")
            t = act.do(lambda e: e.activation(kend, kend, ACT.Exp), t)
            p.note("b read", t)
            kend_done = dve.do(lambda e: e.tensor_tensor(kend, kend, key, ALU.mult), t)
            by = lambda ap: ap.rearrange("p (h c t) -> p h c t", h=4, t=CH)
            dec = lambda ch: by(eb)[:, :, ch, CH - 1:CH].broadcast_to([P, 4, CH])
            for seg, ch in ((0, 3), (1, 2), (3, 1)):
                t = pool.do(lambda e: e.tensor_tensor(qx[:, :, seg, :], by(q)[:, :, ch, :], by(eb)[:, :, ch, :], ALU.mult),
                            e1, "qx read")
            for seg, src, ch in ((2, 0, 2), (4, 1, 1), (5, 2, 1)):
                t = pool.do(lambda e: e.tensor_tensor(qx[:, :, seg, :], qx[:, :, src, :], dec(ch), ALU.mult), t)

            def between(e):
                for h in range(4):
                    out = lambda n, lo, p0: self.b(4 + h // 2, n, (h % 2) * S + lo, p=CH, p0=p0)
                    src = lambda ch: kend[:, h * S + ch * CH:h * S + (ch + 1) * CH]
                    tgt = lambda lo, hi: qx[:, h, lo:hi, :].rearrange("p a b -> p (a b)")
                    e.matmul(out(3 * CH, 0, 0), src(0), tgt(3, 6), start=True, stop=True, skip_group_check=True)
                    e.matmul(out(2 * CH, 0, CH), src(1), tgt(1, 3), start=True, stop=True, skip_group_check=True)
                    last = e.matmul(out(CH, 3 * CH, 0), src(2), tgt(0, 1), start=True, stop=True, skip_group_check=True)
                return last
            t = pe.do(between, kend_done, t, "bank4 read", "bank5 read")
            for name in ("qk0 read", "qk1 read", "qx read"):
                p.note(name, t)
            ps = self.bank[:, 4:6, :].rearrange("p a (h n) -> p (a h) n", n=S)
            cp = comp[:, :, :].rearrange("p (h i) n -> p h i n", i=2)
            lo, hi = slice(0, CH), slice(CH, P)
            dve.do(lambda e: e.memset(sc[hi, :, 0:CH], 0.0), "sc read")
            z = dve.do(lambda e: e.memset(sc[hi, :, 256:320], 0.0))
            act.do(lambda e: e.activation(sc[lo, :, 64:256], ps[lo, :, 0:192], ACT.Copy), t, "sc read")
            act.do(lambda e: e.activation(sc[lo, :, 320:384], ps[lo, :, 192:256], ACT.Copy))
            a = act.do(lambda e: e.activation(sc[hi, :, 128:256], ps[hi, :, 0:128], ACT.Copy))
            p.note("bank4 read", a)
            p.note("bank5 read", a)
            for i in range(2):
                dve.do(lambda e: e.tensor_copy(sc[lo, :, 256 * i:256 * i + 64], cp[lo, :, i, :]), comp_done, "sc read")
                c = dve.do(lambda e: e.tensor_copy(sc[hi, :, 256 * i + 64:256 * i + 128], cp[hi, :, i, :]))
            p.note("comp read", c)

            def outs(e):
                for h in range(4):
                    o = lambda lo, n: self.b(4 + h // 2, n, (h % 2) * S + lo)
                    v = lambda i: proj[:, 26 + 4 * hf + h, i * P:(i + 1) * P]
                    e.matmul(o(0, S), v(0), sc[:, h, 0:S], start=True, stop=False, skip_group_check=True)
                    last = e.matmul(o(P, P), v(1), sc[:, h, S:384], start=False, stop=True, skip_group_check=True)
                return last
            t = pe.do(outs, z, a, c, v_done)
            p.note("sc read", t)
            t = act.do(lambda e: e.activation(q, self.bank[:, 4:6, :].rearrange("p a b -> p (a b)"), ACT.Copy), t)
            p.note("bank4 read", t)
            p.note("bank5 read", t)
        for hf in range(2):
            o = flat(proj[:, 10 + 4 * hf:14 + 4 * hf, :])
            sq = qk[:, 0, :]
            t = act.do(lambda e: e.activation(sq, o, ACT.Square), t, "qk0 read")

            def sums(e):
                for j in range(2):
                    last = e.matmul(self.b(j, 512), self.C("ones"), sq[:, j * 512:(j + 1) * 512], start=True, stop=True)
                return last
            m = pe.do(sums, t, "bank0 read", "bank1 read")
            p.note("qk0 read", m)
            rs = qk[:, 1, :]
            t = act.do(lambda e: e.activation(rs, self.bank[:, 0:2, :].rearrange("p a b -> p (a b)"), ACT.Sqrt,
                                              bias=self.col[:, 0:1], scale=1.0 / P), m, "rs used")
            p.note("bank0 read", t)
            p.note("bank1 read", t)
            d = dve.do(lambda e: e.reciprocal(rs, rs), t)
            d = dve.do(lambda e: e.tensor_tensor(o, o, rs, ALU.mult), d)
            p.note("rs used", d)
            d = dve.do(lambda e: e.scalar_tensor_tensor(out=o, in0=o, scalar=self.vec[:, 1, 54:55],
                                                        in1=flat(proj[:, 34 + 4 * hf:38 + 4 * hf, :]), op0=ALU.mult,
                                                        op1=ALU.mult), d)

    def second_block(self, w_in, w_out, w_gla, w_gla_out):
        p, pe, act, dve, y = self.p, self.pe, self.act, self.dve, self.y
        proj = self.proj = self.sb("proj2", [P, 48, T2], at=self.big)
        y2 = self.y = self.sb("y2", [P, KT, T2], at=self.big)

        def project_body(w, it, side=None, finish=None, each=None):
            slots = [self.load_columns(w, (it * 4 + j) * 256) for j in range(4)]
            for j in range(4):
                banks = (2 * (j % 2), 2 * (j % 2) + 1)
                done = self.unit(slots[j], self.plan([self.b(i) for i in banks], T2), slots[(j + 1) % 4], j == 3,
                                 free=[f"bank{i} read" for i in banks], ready=self.READY,
                                 between=side and (lambda q: side(j, q)))
                tiles = []
                for i in range(2):
                    tiles.append(dve.do(lambda e: e.tensor_tensor(flat(proj[:, bass.ds((it * 4 + j) * 2 + i, 1), :]),
                                                                  self.b(banks[i]), self.rs2[:, :], ALU.mult), done))
                    p.note(f"bank{banks[i]} read", tiles[i])
                if each:
                    each(j, tiles)
            if finish:
                finish()
            p.note("operand free", done)

        dve.wait(self.rs2_done)
        def silu(it):
            def each(j, tiles):
                for u in range(2):
                    x = flat(proj[:, bass.ds((it * 4 + j) * 2 + 32 + u, 1), :])
                    act.do(lambda e: e.activation(x, x, ACT.Silu), tiles[u])
            return each
        self.rt = self.sb("rt", [P, 2, T2], at=self.big + 52224)
        self.rsh = self.sb("rsh", [P, 2, T2], at=self.big + 54400)

        def with_rope(it, gain):
            stages = self.rope2(it, gain)
            project_body(w_in, it, *stages)
        p.repeat(2, lambda it: with_rope(it, self.vec[:, 1, 52:53]))
        with_rope(2, self.vec[:, 1, 53:54])
        project_body(w_in, 3)
        p.repeat(2, lambda it: project_body(w_in, it + 4, each=silu(it)))
        self.join()
        self.attention2()
        self.join()
        for kt in range(KT):
            h = act.do(lambda e: e.activation(self.ah[:, kt, :], proj[:, kt, :], ACT.Copy))
            t = dve.do(lambda e: e.tensor_tensor(self.al[:, kt, :], proj[:, kt, :], self.ah[:, kt, :].bitcast(F32),
                                                 ALU.subtract), h)
            if kt % 2:
                p.note(f"operand {kt // 2}", t)
        summed = self.to_y(w_out, T2)
        rs = self.residual(T2, T2, y2, self.vec[:, 1, 0:16], summed, gain=self.vec[:, 0, 112:128])
        dve.wait(rs)
        pe.wait(*self.READY)

        pe.wait(Token(self.low_in, self.low_in.count, None), self.wlr_zero)

        def low_rank(e):
            for kt in range(KT):
                for a in (self.ah, self.al):
                    last = e.matmul(self.b(5, p=48), self.wlr[:, kt, :], a[:, kt, :].bitcast(F32),
                                    start=kt == 0 and a is self.ah, stop=kt == KT - 1 and a is self.al,
                                    skip_group_check=True)
            return last
        lr = self.lr = self.sb("lr", [48, T2], at=self.work + 4096)
        t = pe.do(low_rank, "bank5 read")
        self.lr_done = dve.do(lambda e: e.tensor_tensor(lr[:, :], self.b(5, p=48), self.rs2[0:48, :], ALU.mult), t,
                              *[f"sq{i} read" for i in range(4)])
        exponents, sums = self.gla_gates()
        p.repeat(2, lambda it: project_body(w_gla, it, lambda j, q: exponents(it, j, q)))
        p.repeat(2, lambda it: project_body(w_gla, it + 2, lambda j, q: sums(it, j, q)))
        p.repeat(2, lambda it: project_body(w_gla, it + 4, each=silu(it)))
        self.join()
        self.gla()
        summed = self.to_y(w_gla_out, T2, last=True)
        r = self.rstd(6, S, D, self.rs[:, 0:S], summed)
        self.x_tile = []
        for kt in range(KT):
            tmp = self.t4[:, kt % 4, 0:S]
            f = dve.do(lambda e: e.scalar_tensor_tensor(out=tmp, in0=y2[:, kt, 0:S], scalar=self.vec[:, 1, 16 + kt:17 + kt],
                                                        in1=self.rs[:, 0:S], op0=ALU.mult, op1=ALU.mult),
                       r, f"t4-{kt % 4} read")
            self.x_tile.append(self.pool.do(lambda e: e.tensor_tensor(self.X[:, kt, 0:S], self.X[:, kt, 0:S], tmp, ALU.add), f))
            p.note(f"t4-{kt % 4} read", self.x_tile[-1])

    def rope2(self, it, gain):
        p, pe, act, dve, pool, proj = self.p, self.pe, self.act, self.dve, self.pool, self.proj
        tile = lambda j, u: flat(proj[:, bass.ds((it * 4 + j) * 2 + u, 1), :])
        buf = lambda j, u: 2 * (j % 2) + u
        made = {}

        def operands(j, tiles):
            for u in range(2):
                n = buf(j, u)
                a = act.do(lambda e: e.activation(self.sq[:, n, :], tile(j, u), ACT.Square), tiles[u], f"hsq{n} read")
                b = act.do(lambda e: e.activation(self.t4[:, n, :], tile(j, u), ACT.Copy, scale=gain), f"xg{n} read")
                made[j, u] = (a, b)
            if j:
                products(j - 1)

        def products(j):
            for u in range(2):
                n, (a, b) = buf(j, u), made[j, u]
                m = pe.do(lambda e: e.matmul(self.b(4 + u), self.C("ones"), self.sq[:, n, :], start=True, stop=True),
                          a, f"bank{4 + u} read")
                p.note(f"hsq{n} read", m)
                w = pe.do(lambda e: e.matmul(self.b(6 + u), self.C("rot2"), self.t4[:, n, :], start=True, stop=True), b,
                          f"bank{6 + u} read")
                made[j, u] = (m, w)

        def turn_start(j, u):
            (m, w), g = made[j, u], self.t4[:, buf(j, u), :]
            t = act.do(lambda e: e.activation(self.rsh[:, u, :], self.b(4 + u), ACT.Sqrt, bias=self.col[:, 0:1],
                                              scale=1.0 / P), m, f"rsh{u} read")
            p.note(f"bank{4 + u} read", t)
            c = pool.do(lambda e: e.tensor_tensor(g, g, self.C("cos2"), ALU.mult), w)
            d = dve.do(lambda e: e.tensor_tensor(self.rt[:, u, :], self.b(6 + u), self.C("sin2"), ALU.mult), w,
                       f"rsh{u} read")
            p.note(f"bank{6 + u} read", d)
            made[j, u] = (t, c, d)

        def turn_end(j, u):
            (t, c, d), n = made[j, u], buf(j, u)
            r, s = self.rt[:, u, :], self.rsh[:, u, :]
            i = dve.do(lambda e: e.reciprocal(s, s), t)
            d = dve.do(lambda e: e.tensor_tensor(r, r, self.t4[:, n, :], ALU.add), c, d)
            p.note(f"xg{n} read", d)
            d = dve.do(lambda e: e.tensor_tensor(tile(j, u), r, s, ALU.mult), d, i)
            p.note(f"rsh{u} read", d)

        def side(j, q):
            if j >= 2:
                if q in (1, 3):
                    turn_start(j - 2, q // 2)
                if q in (3, 5):
                    turn_end(j - 2, q // 2 - 1)

        def finish():
            for j in (2, 3):
                if j == 3:
                    products(3)
                for u in range(2):
                    turn_start(j, u)
                for u in range(2):
                    turn_end(j, u)
        return side, finish, operands

    def attention2(self):
        p, pe, act, dve, pool, proj = self.p, self.pe, self.act, self.dve, self.pool, self.proj
        at = self.ah_at

        def sb(name, shape):
            nonlocal at
            r = self.sb(name, shape, at=at)
            at += 4 * int(np.prod(shape[1:]))
            assert at <= self.ah_at + 2 * 4 * KT * T2
            return r
        qs, ks, vs = sb("qs", [P, 2, 2, T2]), sb("ks", [P, 2, T2]), sb("vs", [P, T2])
        vt, pm, pl = sb("vt2", [P, 2, 3, P]), sb("pm2", [P, 2, 4, T2]), sb("pl2", [32, 2, T2])
        pt, st, qm = sb("pt2", [P, 3, 544]), sb("st2", [P, 2, 4, 8]), sb("qm", [P, 2, 2, META])
        scale = P ** -0.5
        toks = (P, P, META)

        def weights(i, u):
            q = pool.do(lambda e: e.tensor_copy(flat(qs[:, u, :, :]), flat(proj[:, bass.ds(i * 2, 2), :])), f"qs{u} read")
            pool.do(lambda e: e.tensor_copy(qm[:, u, :, :], proj[:, bass.ds(i * 2, 2), S:T2]), f"qs{u} read")
            pool.do(lambda e: e.tensor_copy(ks[:, u, :], flat(proj[:, bass.ds(i + 16, 1), :])))
            v = pool.do(lambda e: e.tensor_copy(vs[:, :], flat(proj[:, bass.ds(i + 24, 1), :])), "vs read")

            def v_turn(e):
                for j, n in enumerate(toks):
                    last = e.transpose(self.b(3, P, j * P, p=n), vs[:, j * P:j * P + n], self.C("ident"))
                return last
            t = pe.do(v_turn, v, "bank3 read")
            p.note("vs read", t)
            act.do(lambda e: e.activation(flat(vt[:, u, 0:2, :]), self.b(3, 2 * P), ACT.Copy), t, f"vt{u} read")
            t = act.do(lambda e: e.activation(vt[0:META, u, 2, :], self.b(3, P, 2 * P, p=META), ACT.Copy))
            p.note("bank3 read", t)
            p.note(f"vt{u} made", t)

            def divide(rec, sm, dst, rows, exp_done):
                r = dve.do(lambda e: e.reciprocal(rec, sm), exp_done)
                return pool.do(lambda e: e.tensor_tensor(dst, dst, rec.broadcast_to([rows, T2]), ALU.mult), r)
            waiting = None
            for n in range(5):
                bank = n % 3
                rows = P if n < 4 else 32
                lhs = qs[:, u, n // 2, (n % 2) * P:(n % 2) * P + P] if n < 4 else flat(qm[:, u, :, :])
                t = pe.do(lambda e: e.matmul(self.b(bank, p=rows), lhs, ks[:, u, :], start=True, stop=True), v,
                          f"bank{bank} read")
                mx, neg, sm, rec = (st[0:rows, u, j, n:n + 1] for j in range(4))
                t = dve.do(lambda e: e.tensor_reduce(mx, self.b(bank, p=rows), AX.X, ALU.max), t)
                t = dve.do(lambda e: e.tensor_scalar(neg, mx, -scale, None, ALU.mult), t)
                dst = pm[:, u, n, :] if n < 4 else pl[:, u, :]
                t = act.do(lambda e: e.activation(dst, self.b(bank, p=rows), ACT.Exp, bias=neg, scale=scale,
                                                  accum_out=sm), t, f"pm{u} turned")
                p.note(f"bank{bank} read", t)
                if waiting:
                    divide(*waiting)
                waiting = (rec, sm, dst, rows, t)
            last = divide(*waiting)
            p.note(f"qs{u} read", Token(pe.done, pe.done.count, p.loop))
            p.note(f"weights{u} made", last)

        def values(i, u):
            def turn(j, bank):
                def products(e):
                    for n in range(4):
                        last = e.transpose(self.b(bank, P, n * P, p=toks[j]), pm[:, u, n, j * P:j * P + toks[j]],
                                           self.C("ident"))
                    return last
                return products

            def turn_meta(e):
                for j in range(3):
                    last = e.transpose(self.b(3, 32, j * 32, p=toks[j]), pl[:, u, j * P:j * P + toks[j]],
                                       self.cs[0:32, self.cat["ident"][0]:self.cat["ident"][0] + 32])
                return last
            pe.wait(f"weights{u} made")
            t = pe.do(turn_meta, "bank3 read")
            act.do(lambda e: e.activation(pt[:, 0:2, 512:544], self.b(3, 64).rearrange("p (a b) -> p a b", a=2),
                                          ACT.Copy), t, "pt read")
            t = act.do(lambda e: e.activation(pt[0:META, 2, 512:544], self.b(3, 32, 64, p=META), ACT.Copy))
            p.note("bank3 read", t)
            for j in range(3):
                bank, rows = 4 + j % 2, toks[j]
                t = pe.do(turn(j, bank), f"bank{bank} read")
                if j == 2:
                    p.note(f"pm{u} turned", t)
                if j == 1:
                    dve_t = dve.do(lambda e: e.tensor_copy(pt[:, 1, 0:512], self.b(bank, 512)), t, "pt read")
                    p.note(f"bank{bank} read", dve_t)
                else:
                    t = act.do(lambda e: e.activation(pt[0:rows, j, 0:512], self.b(bank, 512, p=rows), ACT.Copy), t)
                    p.note(f"bank{bank} read", t)

            def outs(e):
                for bank, lo, hi in ((6, 0, 512), (7, 512, 544)):
                    for j in range(3):
                        last = e.matmul(self.b(bank, hi - lo), vt[0:toks[j], u, j, :], pt[0:toks[j], j, lo:hi],
                                        start=j == 0, stop=j == 2, skip_group_check=True)
                return last
            t = pe.do(outs, t, dve_t, f"vt{u} made", "bank6 read", "bank7 read")
            p.note("pt read", t)
            p.note(f"vt{u} read", t)
            for bank, lo, hi in ((6, 0, S), (7, S, T2)):
                t = dve.do(lambda e: e.tensor_tensor(proj[:, bass.ds(i * 2, 2), lo:hi],
                                                     self.b(bank, 2 * (hi - lo)).rearrange("p (a b) -> p a b", a=2),
                                                     proj[:, bass.ds(i * 2 + 32, 2), lo:hi], ALU.mult), t)
            p.note("bank6 read", t)
            p.note("bank7 read", t)

        weights(0, 0)

        def body(it):
            weights(it * 2 + 1, 1)
            values(it * 2, 0)
            weights(it * 2 + 2, 0)
            values(it * 2 + 1, 1)
        p.repeat(3, body)
        weights(7, 1)
        values(6, 0)
        values(7, 1)

    def gla_gates(self):
        p, pe, act, dve, pool = self.p, self.pe, self.act, self.dve, self.pool
        gates = self.gates = self.sb("gates", [P, 16, T2], at=self.big + 52224)
        mask = self.rs
        for d in range(2):
            for j in range(8):
                bank = j % 4
                t = pe.do(lambda e: e.matmul(self.b(bank), self.up[32 * d:32 * d + 16, j * P:(j + 1) * P],
                                             self.lr[32 * d:32 * d + 16, :], start=True, stop=True), f"bank{bank} read", self.lr_done)
                n, i = 8 * d + j, 32 + 8 * d + j
                t = dve.do(lambda e: e.tensor_scalar(gates[:, n, :], self.b(bank), self.vec[:, 1, i:i + 1], None,
                                                     ALU.add), t)
                p.note(f"bank{bank} read", t)
        self.join()
        t = pool.do(lambda e: e.memset(mask[:, :], 1.0))
        t = pool.do(lambda e: e.memset(mask[:, :].rearrange("p (c n) -> p c n", n=16)[:, 0:17:4, 0:1], 0.0), t)
        dve.wait(t)
        pair = lambda it, j: gates[:, bass.ds((it * 4 + j) * 2, 2), :]
        state = {}

        def exponents(it, j, q):
            t2 = self.t4[:, 2 * (j % 2):2 * (j % 2) + 2, :]
            if q == 1:
                t = act.do(lambda e: e.activation(t2, pair(it, j), ACT.Abs), f"gate{j % 2} made")
                state[j] = act.do(lambda e: e.activation(t2, t2, ACT.Exp, scale=-1.0), t)
            elif q == 3:
                state[j] = act.do(lambda e: e.activation(t2, t2, ACT.Ln, bias=self.col[:, 1:2]), state[j])
            elif q == 5:
                t = dve.do(lambda e: e.scalar_tensor_tensor(out=pair(it, j), in0=pair(it, j), scalar=0.0, in1=t2,
                                                            op0=ALU.min, op1=ALU.subtract), state[j])
                p.note(f"gate{j % 2} made", t)

        def sums(it, j, q):
            if j % 2 == 0 and q == 0:
                dve.wait("gate0 made", "gate1 made")
            n = it * 4 + j
            tile = lambda n: flat(gates[:, bass.ds(n, 1), :])
            tt = self.t4[:, j % 2, :]
            if q == 1:
                dve.do(lambda e: e.tensor_tensor_scan(tile(n), mask[:, :], tile(n), 0.0, ALU.mult, ALU.add))
            elif q == 3:
                state[j] = dve.do(lambda e: e.tensor_tensor_scan(tt, mask[:, :], tile(n + 8), 0.0, ALU.mult, ALU.add),
                                  f"tt{j % 2} read")
            elif q == 4:
                state[j] = pool.do(lambda e: e.tensor_tensor(tile(n + 8), tile(n + 8), tt, ALU.subtract), state[j])
            elif q == 6:
                x4 = lambda ap: ap[:, 0:S].rearrange("p (c n) -> p c n", n=CH)
                dve.do(lambda e: e.tensor_tensor(x4(tile(n + 8)), x4(tile(n + 8)),
                                                 x4(tt)[:, :, CH - 1:CH].broadcast_to([P, NCH, CH]), ALU.add), state[j])
                t = dve.do(lambda e: e.tensor_tensor(tile(n + 8)[:, S:T2], tile(n + 8)[:, S:T2],
                                                     tt[:, T2 - 1:T2].broadcast_to([P, META]), ALU.add))
                p.note(f"tt{j % 2} read", t)
        return exponents, sums

    def gla(self):
        p, pe, act, dve, pool, proj = self.p, self.pe, self.act, self.dve, self.pool, self.proj
        gf, gb = self.gates[:, 0:8, :], self.gates[:, 8:16, :]
        A = self.ah_at
        ex = self.sb("ex", [P, 4, 2, T2], at=A)
        vv = self.sb("vv", [P, 3, 512], at=A + 8704)
        F = self.sb("F", [P, 2, 656], at=A + 14848)
        G = self.sb("G", [P, 2, 512], at=A + 20096)
        sc = self.sb("sc2", [P, 3, T2], at=A + 24192)
        vs = self.sb("vs2", [P, 4, T2], at=A + 27456)
        kend = self.sb("kend", [P, 2, 2, T2], at=self.tmp_at)
        chunk = [(c * CH, CH) for c in range(NCH)] + [(S, META)]
        f_at = {3: 0, 2: 64, 1: 192, 0: 384, 4: 640}
        g_at = {4: 0, 0: 32, 1: 176, 2: 384, 3: 448}
        r = 1.0 / 16

        df = lambda c: ex[:, 0, :, chunk[c][0] + chunk[c][1] - 1:chunk[c][0] + chunk[c][1]]
        db = lambda c: ex[:, 2, :, chunk[c][0]:chunk[c][0] + 1]
        kf, kb = ex[:, 1, :, :], ex[:, 3, :, :]

        def front(h):
            two = lambda ap, t0: ap[:, bass.ds(h * 2 + t0, 2), :]
            k = two(proj, 8)
            e1 = act.do(lambda e: e.activation(ex[:, 0, :, :], two(gf, 0), ACT.Exp, scale=r), "ex read")
            e3 = act.do(lambda e: e.activation(ex[:, 1, :, :], two(gf, 0), ACT.Exp, scale=-r), "heads' keys read")
            e2 = act.do(lambda e: e.activation(ex[:, 2, :, :], two(gb, 0), ACT.Exp, scale=r))
            e4 = act.do(lambda e: e.activation(ex[:, 3, :, :], two(gb, 0), ACT.Exp, scale=-r))
            dve.wait(e4)
            pool.wait(e4)
            a = dve.do(lambda e: e.tensor_tensor(kf, kf, k, ALU.mult))
            b = pool.do(lambda e: e.tensor_tensor(kb, kb, k, ALU.mult))
            dve.wait(a, b, "heads' keys read")
            for d, kk, dec in ((0, kf, df), (1, kb, db)):
                for c in range(5):
                    lo, n = chunk[c]
                    if (d, c) in ((0, 3), (1, 4)):
                        continue
                    t = dve.do(lambda e: e.tensor_tensor(kend[:, d, :, lo:lo + n], kk[:, :, lo:lo + n],
                                                         dec(c).broadcast_to([P, 2, n]), ALU.mult))
            k_done = t
            dve.wait("queries read")
            for c in range(5):
                lo, n = chunk[c]
                for arr, off, d in ((F, f_at[c], 0), (G, g_at[c], 2)):
                    for j in range(2):
                        t = dve.do(lambda e: e.scalar_tensor_tensor(
                            out=arr[:, j, off:off + n], in0=flat(proj[:, bass.ds(h * 2 + j, 1), lo:lo + n]), scalar=r,
                            in1=ex[:, d, j, lo:lo + n], op0=ALU.mult, op1=ALU.mult))
            for src, dst, n, c in ((0, 128, 64, 2), (64, 256, 128, 1), (192, 448, 192, 0)):
                t = pool.do(lambda e: e.tensor_tensor(F[:, :, dst:dst + n], F[:, :, src:src + n],
                                                      df(c).broadcast_to([P, 2, n]), ALU.mult), t)
            t2 = None
            for src, dst, n, c in ((0, 16, 16, 0), (16, 96, 80, 1), (96, 240, 144, 2)):
                t2 = pool.do(lambda e: e.tensor_tensor(G[:, :, dst:dst + n], G[:, :, src:src + n],
                                                       db(c).broadcast_to([P, 2, n]), ALU.mult), t2, t)
            p.note("ex read", t2)
            p.note("front made", t2, k_done)

        def body(h, end=False):
            v = pool.do(lambda e: e.tensor_copy(flat(vs[:, :, :]), flat(proj[:, bass.ds(h * 4 + 16, 4), :])), "vs read")
            for j, n in enumerate((P, P, META)):
                def turn(e):
                    for i in range(4):
                        last = e.transpose(self.b(4 + j, P, i * P, p=n), vs[:, i, j * P:j * P + n], self.C("ident"))
                    return last
                t = pe.do(turn, v, f"bank{4 + j} read")
                a = act.do(lambda e: e.activation(vv[0:n, j, :], self.b(4 + j, 512, p=n), ACT.Copy), t, "vv read")
                p.note(f"bank{4 + j} read", a)
            p.note("vs read", t)
            vv_done = a

            def scores(e):
                def two_tiles(out, key, query):
                    e.matmul(out, key(0), query(0), start=True, stop=False, skip_group_check=True)
                    return e.matmul(out, key(1), query(1), start=False, stop=True, skip_group_check=True)
                for c in range(5):
                    lo, n = chunk[c]
                    p0, bank = (CH * (c % 2), c // 2)
                    o = lambda to, m, bk=bank: self.b(bk, m, to, p=n, p0=p0)
                    key = lambda a, d: (lambda j: a[:, d, j, lo:lo + n])
                    fq = lambda off, m: (lambda j: F[:, j, off:off + m])
                    gq = lambda off, m: (lambda j: G[:, j, off:off + m])
                    two_tiles(o(lo, n), key(ex, 1), fq(f_at[c], n))
                    last = two_tiles(o((c // 2) * CH, n, 3), key(ex, 3), gq(g_at[c], n))
                    if c == 4:
                        last = two_tiles(o(0, S), key(kend, 0), fq(384, 256))
                        continue
                    if c < 3:
                        last = two_tiles(o(lo + CH, S - lo - CH), key(kend, 0), fq((192, 64, 0)[c], S - lo - CH))
                    g0 = (0, 16, 96, 240)[c]
                    last = two_tiles(o(S, META), key(kend, 1), gq(g0, META))
                    if c:
                        last = two_tiles(o(0, lo), key(kend, 1), gq(g0 + META, lo))
                return last
            t = pe.do(scores, "front made", *[f"bank{i} read" for i in range(4)])
            p.note("heads' keys read", t)
            p.note("queries read", t)
            act.do(lambda e: e.activation(sc[:, 0:2, :], self.bank[:, 0:2, 0:T2], ACT.Copy), t, "sc read")
            a = act.do(lambda e: e.activation(sc[0:META, 2, :], self.b(2, p=META), ACT.Copy))
            dve.settle = True
            for c in range(5):
                lo, n = chunk[c]
                rows = slice(CH * (c % 2), CH * (c % 2) + n)
                lo2, hi2 = self.cat["later"]
                t = dve.do(lambda e: e.copy_predicated(sc[rows, c // 2, lo:lo + n],
                                                       self.cs[rows, lo2:lo2 + n].bitcast(U32),
                                                       self.b(3, n, (c // 2) * CH, p=n, p0=CH * (c % 2))), a)
            dve.settle = False
            for i in range(4):
                p.note(f"bank{i} read", t)
            if not end:
                front(h + 1)

            def outs(e):
                for i in range(4):
                    for j, n in enumerate((P, P, META)):
                        last = e.matmul(self.b(4 + i), vv[0:n, j, i * P:(i + 1) * P], sc[0:n, j, :], start=j == 0,
                                        stop=j == 2)
                return last
            t = pe.do(outs, t, vv_done, *[f"bank{4 + i} read" for i in range(4)])
            p.note("sc read", t)
            p.note("vv read", t)
            for i in range(4):
                a = act.do(lambda e: e.activation(self.sq[:, i, :], self.b(4 + i), ACT.Square), t, f"osq{i} read")
                d = dve.do(lambda e: e.tensor_tensor(flat(proj[:, bass.ds(h * 4 + 16 + i, 1), :]), self.b(4 + i),
                                                     flat(proj[:, bass.ds(h * 4 + 32 + i, 1), :]), ALU.mult), a)
                p.note(f"bank{4 + i} read", d)
                m = pe.do(lambda e: e.matmul(self.b(0), self.C("ones"), self.sq[:, i, :], start=i == 0, stop=i == 3), a,
                          *(["bank0 read"] if i == 0 else []))
                p.note(f"osq{i} read", m)
            a = act.do(lambda e: e.activation(flat(proj[:, bass.ds(h * 2, 1), :]), self.b(0), ACT.Copy), m)
            p.note("bank0 read", t, a)
        front(0)
        p.repeat(3, body)
        body(3, end=True)
        self.join()
        sums = proj[:, 0:8:2, :]
        t = act.do(lambda e: e.activation(sums, sums, ACT.Sqrt, bias=self.col[:, 0:1], scale=1.0 / 512))
        r_done = dve.do(lambda e: e.reciprocal(sums, sums), t)
        highs = []

        def low(kt):
            t = dve.do(lambda e: e.tensor_tensor(self.al[:, kt, :], self.t4[:, kt % 4, :],
                                                 self.ah[:, kt, :].bitcast(F32), ALU.subtract), highs[kt])
            p.note(f"t4-{kt % 4} read", t)
            if kt % 2:
                p.note(f"operand {kt // 2}", t)
        for kt in range(KT):
            full = self.t4[:, kt % 4, :]
            t = dve.do(lambda e: e.scalar_tensor_tensor(
                out=full, in0=proj[:, 16 + kt, :], scalar=self.vec[:, 1, 48 + kt % 4:49 + kt % 4],
                in1=proj[:, 2 * (kt // 4), :], op0=ALU.mult, op1=ALU.mult), r_done, f"t4-{kt % 4} read")
            highs.append(act.do(lambda e: e.activation(self.ah[:, kt, :], full, ACT.Copy), t))
            if kt >= 2:
                low(kt - 2)
        low(KT - 2)
        low(KT - 1)

    def finish(self, out):
        p, pe, act, dve, sp = self.p, self.pe, self.act, self.dve, self.sp
        rows = self.sb("out_rows", [P, 2, D], at=self.big + 20000 // 32 * 32)
        stored = p.counter("out_stored")
        view = out[0].rearrange("(i p) d -> p i d", p=P)
        for g in range(4):
            for i in range(2):
                bank = (2 * g + i) % 6

                def turn(e):
                    for j in range(4):
                        last = e.transpose(self.b(bank, P, j * P), self.X[:, 4 * g + j, i * P:(i + 1) * P], self.C("ident"))
                    return last
                t = pe.do(turn, f"bank{bank} read", self.x_tile[4 * g + 3])
                if i:
                    t = dve.do(lambda e: e.tensor_copy(rows[:, i, g * 512:(g + 1) * 512], self.b(bank, 512)), t)
                else:
                    t = act.do(lambda e: e.activation(rows[:, i, g * 512:(g + 1) * 512], self.b(bank, 512), ACT.Copy), t)
                p.note(f"bank{bank} read", t)
                sp.do(lambda e: e.dma_start(view[:, i, g * 512:(g + 1) * 512], rows[:, i, g * 512:(g + 1) * 512]), t,
                      counter=stored, add=16)
        sp.wait(Token(stored, stored.count, None))


_INS = ['x', 'c', 'positions', 'w_ada', 'b_ada', 'g_pre_mix', 'g_post_mix', 'g_pre_ffn', 'g_post_ffn', 'w_in',
        'attn_sinks', 'w_attn_proj', 'hg_lower_bounds', 'hg_norm', 'w_hgrn_proj', 'w_out', 'w_ffn_in', 'w_ffn_out',
        'meta_tokens_2', 'pre_norm_2', 'post_norm_2', 'attn_w_in_2', 'attn_q_norm_2', 'attn_k_norm_2',
        'attn_w_out_2', 'gla_w_in_2', 'gla_gk_up_2', 'gla_gk_bias_2', 'gla_o_norm_2', 'gla_w_out_2']


def kernel(**inputs):
    import concourse.bacc as _bacc
    from concourse.bass_utils import run_bass_kernel_spmd as _run

    nc = _bacc.Bacc("TRN2", target_bir_lowering=False, num_devices=1, dynamic_dma_scratch_size=1024)
    arrays, args = {}, []
    for name in _INS:
        arrays[f"in_{name}_dram"] = np.ascontiguousarray(inputs[name])
    arrays["consts_dram"] = const_tables()[1]
    for name, a in arrays.items():
        args.append(nc.dram_tensor(name, a.shape, mybir.dt.from_np(a.dtype), kind="ExternalInput").ap())
    args.append(nc.dram_tensor("out_0_dram", (1, S, D), F32, kind="ExternalOutput").ap())
    build(nc, *args)
    r = _run(nc, [arrays], core_ids=[0])
    return r.results[0]["out_0_dram"]
```
